# Optimizing a Trainium2 kernel written in Bass

```python
import math
import jax, jax.numpy as jnp
from jax import lax
import numpy as np

D_MODEL = 1024
BATCH = 1
SEQ = 1024
DEPTH = 2

N_MIXERS = 2
N_ATTN_LAYERS = (DEPTH + 1) // 2
N_POOL_LAYERS = DEPTH // 2
EPS = 1e-6
HEAD_DIM = 64
N_HEADS = D_MODEL // (2 * HEAD_DIM)
ATTN_WIDTH = N_HEADS * 2 * HEAD_DIM
Q_BLOCK = 128
NUM_BUCKETS = 32
MAX_EXACT = NUM_BUCKETS // 2
MAX_DISTANCE = 128
POOL_WINDOWS = (2, 4, 8, 16)
N_POOL_GROUPS = len(POOL_WINDOWS)
GROUP_WIDTH = D_MODEL // N_POOL_GROUPS
N_EXPERT_GROUPS = 4
EXPERTS_PER_GROUP = 8
N_EXPERTS = N_EXPERT_GROUPS * EXPERTS_PER_GROUP
TOP_K = 2
EXPERT_FF = D_MODEL // 2
EXPERT_BLOCK = 128

kernel_name = "hybrid_diffattn_pool_hmoe"

def rms_norm(x, gain):
    xf = x.astype(jnp.float32)
    y = xf * lax.rsqrt(jnp.mean(xf * xf, axis=-1, keepdims=True) + EPS)
    return (y * gain.astype(jnp.float32)).astype(x.dtype)

def rel_bucket(dist):
    n = jnp.maximum(dist, 0)
    nf = jnp.maximum(n, 1).astype(jnp.float32)
    large = MAX_EXACT + (jnp.log(nf / MAX_EXACT) / math.log(MAX_DISTANCE / MAX_EXACT)
                         * (NUM_BUCKETS - MAX_EXACT)).astype(jnp.int32)
    large = jnp.minimum(large, NUM_BUCKETS - 1)
    return jnp.where(n < MAX_EXACT, n, large)

def diff_attention(h, w_qkv, q_gain, k_gain, lq1, lk1, lq2, lk2, subln_gain, w_o, rel_bias, lambda_init):
    B, S, _ = h.shape
    qkv = h @ w_qkv
    q, k, v = jnp.split(qkv, 3, axis=-1)
    q = rms_norm(q.reshape(B, S, N_HEADS, 2, HEAD_DIM), q_gain) * (HEAD_DIM ** -0.5)
    k = rms_norm(k.reshape(B, S, N_HEADS, 2, HEAD_DIM), k_gain)
    v = v.reshape(B, S, N_HEADS, 2 * HEAD_DIM)
    lam = (jnp.exp(jnp.sum(lq1.astype(jnp.float32) * lk1.astype(jnp.float32)))
           - jnp.exp(jnp.sum(lq2.astype(jnp.float32) * lk2.astype(jnp.float32))) + lambda_init)
    n_blk = S // Q_BLOCK
    qb = q.reshape(B, n_blk, Q_BLOCK, N_HEADS, 2, HEAD_DIM).transpose(1, 0, 2, 3, 4, 5)
    k_pos = jnp.arange(S)

    def one_block(args):
        qi, bi = args
        q_pos = bi * Q_BLOCK + jnp.arange(Q_BLOCK)
        dist = q_pos[:, None] - k_pos[None, :]
        bias = rel_bias.astype(jnp.float32)[rel_bucket(dist)].transpose(2, 0, 1)
        logits = jnp.einsum('bqhcd,bkhcd->bhcqk', qi, k).astype(jnp.float32) + bias[None, :, None]
        logits = jnp.where((dist >= 0)[None, None, None], logits, -jnp.inf)
        p = jax.nn.softmax(logits, axis=-1)
        a = p[:, :, 0] - lam * p[:, :, 1]
        return jnp.einsum('bhqk,bkhe->bqhe', a.astype(v.dtype), v)

    o = lax.map(one_block, (qb, jnp.arange(n_blk)))
    o = o.transpose(1, 0, 2, 3, 4).reshape(B, S, N_HEADS, 2 * HEAD_DIM)
    o = rms_norm(o, subln_gain) * (1.0 - lambda_init)
    return o.reshape(B, S, ATTN_WIDTH) @ w_o

def multiscale_pool(h, w_in, w_group, w_out, scale):
    B, S, _ = h.shape
    u = (h @ w_in).reshape(B, S, N_POOL_GROUPS, GROUP_WIDTH)
    uf = u.astype(jnp.float32)
    csum = jnp.cumsum(uf, axis=1)
    pos1 = jnp.arange(1, S + 1)
    outs = []
    for g, w in enumerate(POOL_WINDOWS):
        c = csum[:, :, g]
        shifted = jnp.pad(c, ((0, 0), (w, 0), (0, 0)))[:, :S]
        cnt = jnp.minimum(pos1, w).astype(jnp.float32)[None, :, None]
        outs.append((c - shifted) / cnt - uf[:, :, g])
    pooled = jnp.stack(outs, axis=2).astype(h.dtype)
    mixed = jnp.einsum('bsgc,gce->bsge', pooled, w_group).reshape(B, S, D_MODEL)
    return (mixed @ w_out) * scale

def routed_experts(xf, expert, weight, w_gate, w_up, w_down):
    T, D = xf.shape
    A = T * TOP_K
    e_flat = expert.reshape(A)
    tok = jnp.arange(A, dtype=jnp.int32) // TOP_K
    wt = weight.reshape(A)
    order = jnp.argsort(e_flat)
    e_sorted = e_flat[order]
    counts = jnp.bincount(e_flat, length=N_EXPERTS)
    padded = (counts + EXPERT_BLOCK - 1) // EXPERT_BLOCK * EXPERT_BLOCK
    pad_end = jnp.cumsum(padded)
    pad_start = pad_end - padded
    start = jnp.cumsum(counts) - counts
    dest = pad_start[e_sorted] + jnp.arange(A) - start[e_sorted]
    n_blocks = -(-A // EXPERT_BLOCK) + N_EXPERTS
    P = n_blocks * EXPERT_BLOCK
    slot_tok = jnp.full((P,), T, jnp.int32).at[dest].set(tok[order])
    slot_w = jnp.zeros((P,), jnp.float32).at[dest].set(wt[order])
    block_expert = jnp.minimum(
        jnp.searchsorted(pad_end, jnp.arange(n_blocks) * EXPERT_BLOCK, side='right'), N_EXPERTS - 1)
    x_pad = jnp.concatenate([xf, jnp.zeros((1, D), xf.dtype)], axis=0)
    xb = x_pad[slot_tok].reshape(n_blocks, EXPERT_BLOCK, D)

    def expert_block(args):
        xe, e = args
        return (jax.nn.silu(xe @ w_gate[e]) * (xe @ w_up[e])) @ w_down[e]

    yb = lax.map(expert_block, (xb, block_expert)).reshape(P, D)
    out = jnp.zeros((T + 1, D), jnp.float32).at[slot_tok].add(yb.astype(jnp.float32) * slot_w[:, None])
    return out[:T].astype(xf.dtype)

def hier_moe(h, wg1, bg1, wg2, bg2, w_gate, w_up, w_down):
    B, S, D = h.shape
    T = B * S
    xf = h.reshape(T, D)
    g_prob = jax.nn.softmax((xf @ wg1).astype(jnp.float32) + bg1.astype(jnp.float32), axis=-1)
    gp, gidx = lax.top_k(g_prob, 1)
    e_logit = ((xf @ wg2).astype(jnp.float32) + bg2.astype(jnp.float32)).reshape(T, N_EXPERT_GROUPS, EXPERTS_PER_GROUP)
    e_sel = jnp.take_along_axis(e_logit, gidx[:, :, None], axis=1)[:, 0]
    ev, eidx = lax.top_k(e_sel, TOP_K)
    weight = jax.nn.softmax(ev, axis=-1) * gp
    expert = gidx * EXPERTS_PER_GROUP + eidx
    return routed_experts(xf, expert, weight, w_gate, w_up, w_down).reshape(B, S, D)

def setup_inputs(seed: int = 0) -> dict:
    key = jax.random.key(seed)
    ks = jax.random.split(key, 32)
    f32 = jnp.float32
    nrm = lambda k, shp, s: jax.random.normal(k, shp, f32) * s
    nA, nP, L = N_ATTN_LAYERS, N_POOL_LAYERS, DEPTH
    return {
        "x": nrm(ks[0], (BATCH, SEQ, D_MODEL), 1.0),
        "rel_bias": nrm(ks[1], (NUM_BUCKETS, N_HEADS), 0.5),
        "attn_norm": 1.0 + nrm(ks[2], (nA, D_MODEL), 0.05),
        "w_qkv": nrm(ks[3], (nA, D_MODEL, 3 * ATTN_WIDTH), D_MODEL ** -0.5),
        "q_gain": 1.0 + nrm(ks[4], (nA, HEAD_DIM), 0.05),
        "k_gain": 1.0 + nrm(ks[5], (nA, HEAD_DIM), 0.05),
        "lambda_q1": nrm(ks[6], (nA, HEAD_DIM), 0.1),
        "lambda_k1": nrm(ks[7], (nA, HEAD_DIM), 0.1),
        "lambda_q2": nrm(ks[8], (nA, HEAD_DIM), 0.1),
        "lambda_k2": nrm(ks[9], (nA, HEAD_DIM), 0.1),
        "subln_gain": 1.0 + nrm(ks[10], (nA, 2 * HEAD_DIM), 0.05),
        "w_o": nrm(ks[11], (nA, ATTN_WIDTH, D_MODEL), ATTN_WIDTH ** -0.5),
        "pool_norm": 1.0 + nrm(ks[12], (nP, D_MODEL), 0.05),
        "pool_w_in": nrm(ks[13], (nP, D_MODEL, D_MODEL), D_MODEL ** -0.5),
        "pool_w_group": nrm(ks[14], (nP, N_POOL_GROUPS, GROUP_WIDTH, GROUP_WIDTH), GROUP_WIDTH ** -0.5),
        "pool_w_out": nrm(ks[15], (nP, D_MODEL, D_MODEL), D_MODEL ** -0.5),
        "pool_scale": 1.0 + nrm(ks[16], (nP, D_MODEL), 0.1),
        "ffn_norm": 1.0 + nrm(ks[17], (L, D_MODEL), 0.05),
        "router_group_w": nrm(ks[18], (L, D_MODEL, N_EXPERT_GROUPS), D_MODEL ** -0.5),
        "router_group_b": nrm(ks[19], (L, N_EXPERT_GROUPS), 0.01),
        "router_expert_w": nrm(ks[20], (L, D_MODEL, N_EXPERTS), D_MODEL ** -0.5),
        "router_expert_b": nrm(ks[21], (L, N_EXPERTS), 0.01),
        "w_gate": nrm(ks[22], (L, N_EXPERTS, D_MODEL, EXPERT_FF), D_MODEL ** -0.5),
        "w_up": nrm(ks[23], (L, N_EXPERTS, D_MODEL, EXPERT_FF), D_MODEL ** -0.5),
        "w_down": nrm(ks[24], (L, N_EXPERTS, EXPERT_FF, D_MODEL), EXPERT_FF ** -0.5),
    }

def reference(x, rel_bias, attn_norm, w_qkv, q_gain, k_gain, lambda_q1, lambda_k1, lambda_q2, lambda_k2,
              subln_gain, w_o, pool_norm, pool_w_in, pool_w_group, pool_w_out, pool_scale,
              ffn_norm, router_group_w, router_group_b, router_expert_w, router_expert_b,
              w_gate, w_up, w_down):
    for i in range(DEPTH):
        j = i // N_MIXERS
        if i % N_MIXERS == 0:
            lambda_init = 0.8 - 0.6 * math.exp(-0.3 * i)
            h = rms_norm(x, attn_norm[j])
            x = x + diff_attention(h, w_qkv[j], q_gain[j], k_gain[j], lambda_q1[j], lambda_k1[j],
                                   lambda_q2[j], lambda_k2[j], subln_gain[j], w_o[j], rel_bias, lambda_init)
        else:
            h = rms_norm(x, pool_norm[j])
            x = x + multiscale_pool(h, pool_w_in[j], pool_w_group[j], pool_w_out[j], pool_scale[j])
        h = rms_norm(x, ffn_norm[i])
        x = x + hier_moe(h, router_group_w[i], router_group_b[i], router_expert_w[i], router_expert_b[i],
                         w_gate[i], w_up[i], w_down[i])
    return x


_drawn_inputs = setup_inputs


def setup_inputs(seed=0):
    import zlib

    import numpy as np

    out = dict(_drawn_inputs(seed))
    spreads = {}
    factors = {'lambda_k2': 3.072, 'router_group_b': 3.118, 'router_expert_b': 3.358}
    for name, (base, spread) in spreads.items():
        noise = np.random.default_rng([zlib.crc32(name.encode()), seed]).standard_normal(out[name].shape)
        drawn = base * np.exp(spread * noise) if base else spread * noise
        out[name] = __import__('jax').numpy.asarray(drawn.astype(out[name].dtype))
    for name, factor in factors.items():
        out[name] = (out[name] * factor).astype(out[name].dtype)
    return out
```

```python
import math
from contextlib import ExitStack

import numpy as np

import concourse.bass as bass
from concourse import mybir

D = 1024
S = 1024
P = 128
NT = S // P
KD = D // P
HEADS = 8
HD = 64
WINDOWS = (2, 4, 8, 16)
PAD = max(WINDOWS)
GROUPS, PER_GROUP = 4, 8
NE = GROUPS * PER_GROUP
FF = D // 2
KF = FF // P
BANK = 512
EPS = 1e-6
LAMBDA_INIT = 0.8 - 0.6 * math.exp(-0.3 * 0)
BIG = 3.0e38
MASKED = -1.0e30
IDX0 = 64.0
NO_SLOT = 1 << 20
BUCKETS = 32
RING = 3
LINE = 3 * P - 1


def rel_bucket(dist):
    n = np.maximum(dist, 0)
    nf = np.maximum(n, 1).astype(np.float32)
    exact = BUCKETS // 2
    large = exact + (np.log(nf / exact) / math.log(128 / exact) * (BUCKETS - exact)).astype(np.int32)
    return np.where(n < exact, n, np.minimum(large, BUCKETS - 1))


C_IDENT, C_TRI, C_IOTA4, C_IOTA32, C_THR, C_CNT, C_FLIP = 0, 128, 256, 260, 292, 299, 363
C_END = C_FLIP + P


def float_constants():
    c = np.zeros((P, C_END), np.float32)
    c[:, C_IDENT:C_IDENT + P] = np.eye(P)
    c[:, C_TRI:C_TRI + P] = np.triu(np.ones((P, P)), 1)
    c[:, C_IOTA4:C_IOTA4 + GROUPS] = np.arange(GROUPS) - IDX0
    c[:, C_IOTA32:C_IOTA32 + NE] = np.arange(NE) - IDX0
    c[:, C_THR:C_THR + 7] = P * np.arange(1, 8)
    c[:, C_FLIP:] = np.eye(P)[::-1]
    for g, w in enumerate(WINDOWS):
        c[:, C_CNT + g * PAD:C_CNT + (g + 1) * PAD] = 1.0 / np.minimum(np.arange(1, PAD + 1), w)
    return c


def bias_line_constants():
    c = np.zeros((P, LINE + 1), np.float32)
    dist = 2 * P - 1 - np.arange(LINE)
    for m, d in enumerate(dist):
        if d >= 0:
            c[rel_bucket(np.array(d)), m] += 1.0
            c[BUCKETS - 1, m] -= 1.0
        else:
            c[BUCKETS, m] = 1.0
    return c


def int_constants():
    t = np.arange(NT)[None, :] * P + np.arange(P)[:, None]
    return (2 * t[:, :, None] + np.arange(2)).reshape(P, 2 * NT).astype(np.int32)


def hybrid_trunk_kernel(nc, t, out):
    f32, i32 = mybir.dt.float32, mybir.dt.int32
    ALU, ACT, AX = mybir.AluOpType, mybir.ActivationFunctionType, mybir.AxisListType
    ds = bass.ds
    ctx = ExitStack()
    with ctx:
        def sb(name, shape, dt=f32):
            return ctx.enter_context(nc.sbuf_tensor(name, shape, dt))

        def sem(name):
            return ctx.enter_context(nc.semaphore(name))

        def dram(name, shape, dt=f32):
            return nc.dram_tensor(name, shape, dt, kind="Internal")

        def row_of(ap, n, offset=0):
            return bass.AP(tensor=ap.tensor, offset=offset, ap=[[0, P], [1, n]])

        line_dram = dram("bias_line", (HEADS, LINE + 1))
        normed_dram = [dram(f"normed_{l}", (S, D)).ap() for l in range(2)]
        slots_dram = [dram(f"slots_{l}", (S * NE, 1), i32) for l in range(2)]
        expert_out_dram = [dram(f"expert_out_{l}", (2 * S, D)).ap() for l in range(2)]

        X0, R1, R2, R3, R4, END = 0, 8192, 16384, 32768, 40960, 51200
        arena = sb("arena", [P, END])

        def view(off, *dims, dt=f32):
            n = int(np.prod(dims))
            assert off + n <= END
            ap = arena[:, off:off + n]
            if dt != f32:
                ap = ap.bitcast(dt)
            if len(dims) == 2:
                ap = ap.rearrange("p (a b) -> p a b", a=dims[0])
            if len(dims) == 3:
                ap = ap.rearrange("p (a b c) -> p a b c", a=dims[0], b=dims[1])
            return ap

        x = view(X0, NT, D)
        hT = view(R1, KD, S)
        normed = [view(R4 + 1024 * b, D) for b in range(2)]
        square = view(R4 + 2048, D)
        wqkv_ring = [view(R4 + 4096 * b, KD, BANK) for b in range(2)]
        qk_square = view(R4 + 8192, 8, HD)
        qk_rows = [view(R4 + 8704 + 512 * b, 8, HD) for b in range(2)]
        qkT = view(R2, 2 * HEADS, S)
        v = view(R3, NT, D)
        strip = view(R4, HEADS, 2 * P)
        strip_flipped = view(R1, HEADS, 2 * P)
        q_head = [view(R4 + 2048 + 1024 * b, S) for b in range(2)]
        k_head = [view(R4 + 4096 + 1024 * b, S) for b in range(2)]
        prob0 = [view(R4 + 6144 + 1024 * b, S) for b in range(2)]
        prob1 = view(R4 + 8192, S)
        probT = view(R4 + 9216, NT, P)
        o_rows = view(R2, HEADS, S)
        wo = view(R1, KD, D)
        o_square = view(R4, HEADS, P)
        o_normed = [view(R4 + 1024 + 1024 * b, HEADS, P) for b in range(2)]
        oT = [view(R4 + 3072 + 1024 * b, KD, P) for b in range(2)]
        wslot = [(view(R1 + 12288 * b, KD, FF), view(R1 + 12288 * b + 4096, KD, FF),
                  view(R1 + 12288 * b + 8192, KF, D)) for b in range(RING)]
        E0 = R1 + 12288 * RING
        x_rows = view(E0, D)
        y_rows = view(E0 + 1024, D)
        xT = view(E0 + 2048, KD, P)
        gated = view(E0 + 3072, KF, P)
        hiddenT = view(E0 + 3584, KF, P)
        y_pair = [view(R1 + 2048 * b, 2, D) for b in range(2)]
        rT = [view(R4 + 3072 + 1024 * b, KD, P) for b in range(2)]
        t256 = [view(E0 + 256 * j, NT, NE) for j in range(7)]
        t32 = [view(E0 + 1792 + 32 * j, NT, GROUPS) for j in range(4)]
        logit = view(E0 + 1920, NT, GROUPS + NE)
        w_router = view(E0 + 2208, KD, GROUPS + NE)
        b_router = view(E0 + 2496, GROUPS + NE)
        slot_all = view(E0 + 4096, NT, NE, dt=i32)
        gather_all = view(E0 + 4352, NT, NE, dt=i32)
        no_slots = view(E0 + 4608, 256, dt=i32)
        w_in = view(R2, KD, D)
        w_out = view(R2 + 8192, KD, D)
        UW = PAD + S
        uT = view(R3, KD, UW)
        w_grp = view(R4 + 3072, KD, 2 * P)
        scale_row = view(R4 + 5120, D)
        win = [view(R4 + 6144 + UW * j, UW) for j in range(2)]
        out_scaled = view(R4 + 6144 + 2 * UW, D)
        mixedT = view(R1, KD, S)

        const = sb("const", [P, C_END])
        ident, tri = const[:, C_IDENT:C_IDENT + P], const[:, C_TRI:C_TRI + P]
        assignment = sb("assignment", [P, 2 * NT], i32)
        gains = sb("gains", [P, 4, KD])
        qk_gain = sb("qk_gain", [P, 4])
        sub_gain = sb("sub_gain", [P, 1])
        small = sb("small", [P, 64])
        eps_t = small[:, 0:1]
        neg_lam = small[:, 1:2]
        lam_t = small[:, 2:8]
        ssq, std, rstd = small[:, 8:16], small[:, 16:24], small[:, 24:32]
        neg_max = small[:, 32:36].rearrange("p (a b) -> p a b", a=2)
        sums = small[:, 36:40].rearrange("p (a b) -> p a b", a=2)
        rsum = small[:, 40:44].rearrange("p (a b) -> p a b", a=2)
        coef = small[:, 44:46]
        ones = sb("ones", [P, P])
        t8 = sb("t8", [P, 12, NT])
        gate_w = sb("gate_w", [P, NT, 2])
        dest = sb("dest", [P, NT, 2], i32)
        counts = sb("counts", [P, 4, NE])
        meta = sb("meta", [1, NE, 4], i32)
        total = sb("total", [1, 1], i32)
        gather_now = sb("gather_now", [P, 1], i32)
        scatter_now = sb("scatter_now", [P, 1], i32)
        scatter_next = sb("scatter_next", [P, 1], i32)

        psum = ctx.enter_context(nc.psum_tensor("psum", [P, 8 * BANK], f32))

        def bank(b, n=1):
            return psum[:, BANK * b:BANK * (b + n)]

        phase_done = sem("phase_done")
        x_in, params_in, rel_in = sem("x_in"), sem("params_in"), sem("rel_in")
        rel_zeroed, line_psum, line_sb, line_stored, strip_in = (
            sem(n) for n in ("rel_zeroed", "line_psum", "line_sb", "line_stored", "strip_in"))
        strip_turned, strip_kept = sem("strip_turned"), sem("strip_kept")
        lam_sums, lam_exp = sem("lam_sums"), sem("lam_exp")
        dve_link, act_link = sem("dve_link"), sem("act_link")

        norm_ssq, norm_std, norm_link = sem("norm_ssq"), sem("norm_std"), sem("norm_link")
        norm_rows_ready = [sem(f"norm_rows{b}") for b in range(2)]
        norm_turned = [sem(f"norm_turned{b}") for b in range(2)]
        norm_kept = [sem(f"norm_kept{b}") for b in range(2)]
        NORMS = ["attn", "ffn0", "pool", "ffn1"]
        PAIRS = NT // 2
        wqkv_in = [sem(f"wqkv_in{b}") for b in range(2)]
        qkv_mm, qk_sq, qk_ssq, qk_std, qk_ready, qk_turned, qk_kept, v_kept = (
            sem(n) for n in ("qkv_mm", "qk_sq", "qk_ssq", "qk_std", "qk_ready", "qk_turned", "qk_kept", "v_kept"))
        qk_link = sem("qk_link")
        staged = [sem(f"staged{b}") for b in range(2)]
        scores = [sem(f"scores{c}") for c in range(2)]
        maxed = [sem(f"maxed{c}") for c in range(2)]
        exped = [sem(f"exped{c}") for c in range(2)]
        att_link, combined, p_turned, p_kept, av_done, o_kept = (
            sem(n) for n in ("att_link", "combined", "p_turned", "p_kept", "av_done", "o_kept"))
        wo_in = sem("wo_in")
        o_sq, o_ssq, o_std, o_link = sem("o_sq"), sem("o_ssq"), sem("o_std"), sem("o_link")
        on_ready = [sem(f"on_ready{b}") for b in range(2)]
        o_turned = [sem(f"o_turned{b}") for b in range(2)]
        oT_kept = [sem(f"oT_kept{b}") for b in range(2)]
        proj_mm = [sem(f"proj_mm{b}") for b in range(2)]
        proj_added = [sem(f"proj_added{b}") for b in range(2)]

        router_in, table_cleared, clear_ready, act_in, act_out, masks, ranks, dests, tabled, table_in, lists = (
            sem(n) for n in ("router_in", "table_cleared", "clear_ready", "act_in", "act_out", "masks", "ranks",
                             "dests", "tabled", "table_in", "lists"))
        stored = [sem(f"stored{b}") for b in range(2)]
        logits = [sem(f"logits{b}") for b in range(2)]
        biased = [sem(f"biased{b}") for b in range(2)]
        w_in_sem = [[sem(f"w{k}_in{b}") for b in range(RING)] for k in range(3)]
        pair_in = [sem(f"pair_in{b}") for b in range(2)]
        pair_used = [sem(f"pair_used{b}") for b in range(2)]
        sum_link = sem("sum_link")

        class Moe:
            def __init__(self, l):
                def s(n):
                    return sem(f"moe{l}_{n}")
                self.pool_link = s("pool_link")
                self.rows_in, self.turned, self.xT_kept = s("rows_in"), s("turned"), s("xT_kept")
                self.gate_up, self.silu, self.hidden = s("gate_up"), s("silu"), s("hidden")
                self.down, self.y_kept, self.scattered = s("down"), s("y_kept"), s("scattered")

        moe_of = [Moe(0), Moe(1)]
        pool_in, u_mm, u_kept, pooled, pool_link, mix_mm, mix_kept, out_mm, out_added, out_link, pads = (
            sem(n) for n in ("pool_in", "u_mm", "u_kept", "pooled", "pool_link", "mix_mm", "mix_kept",
                             "out_mm", "out_added", "out_link", "pads"))
        out_stored = sem("out_stored")

        N_PARAMS = 20
        CREDITS = [(s, 1) for s in (norm_ssq, *norm_turned, *norm_kept, *biased, *oT_kept, *proj_added, o_ssq, qk_ssq,
                                    qk_ready)]
        CREDITS += [(s, 16) for s in stored]
        for m in moe_of:
            CREDITS += [(m.y_kept, 1), (m.turned, 1)]
        PH = ["setup", "attn_norm", "qkv", "attention", "projection", "moe0", "pool_norm", "pool", "moe1"]

        def end_phase(eng, name):
            eng.drain().then_inc(phase_done, 1)
            eng.wait_ge(phase_done, 4 * (PH.index(name) + 1))

        def after_phase(eng, name):
            eng.wait_ge(phase_done, 4 * (PH.index(name) + 1))

        class Link:
            def __init__(self, eng, s, base=0):
                self.eng, self.s, self.base, self.n = eng, s, base, 0

            def __call__(self, ins):
                ins.then_inc(self.s, 1)
                self.n += 1
                self.eng.wait_ge(self.s, self.base + self.n)

        block = ctx.enter_context(nc.Block())

        @block.sync
        def _(sp):
            sp.dma_start(x, t["x"][0].rearrange("(t p) d -> p t d", p=P)).then_inc(x_in, 16)
            n_params = [0]

            def param(dst, src):
                sp.dma_start(dst, src, allow_slow_non_contiguous=True).then_inc(params_in, 16)
                n_params[0] += 1

            param(const[:], t["const"])
            param(assignment[:], t["assignment"])
            for j, src in enumerate((t["attn_norm"][0], t["pool_norm"][0], t["ffn_norm"][0], t["ffn_norm"][1])):
                param(gains[:, j, :], src.rearrange("(k p) -> p k", p=P))
            for c in range(2):
                for n in range(4):
                    param(qk_gain[HD * c:HD * (c + 1), n:n + 1],
                          t["q_gain" if n < 2 else "k_gain"][0].rearrange("(p a) -> p a", a=1))
            param(sub_gain[:], t["subln_gain"][0].rearrange("(p a) -> p a", a=1))
            for j, n in enumerate(("lambda_q1", "lambda_k1", "lambda_q2", "lambda_k2")):
                param(view(R4 + 64 * j, HD), row_of(t[n], HD))
            param(view(R4 + 512, LINE + 1), t["bias_line"])
            assert n_params[0] == N_PARAMS
            sp.wait_ge(rel_zeroed, 2)
            sp.dma_start(arena[0:BUCKETS, R4 + 1024:R4 + 1024 + HEADS], t["rel_bias"]).then_inc(rel_in, 16)
            sp.wait_ge(line_sb, 1)
            sp.dma_start(line_dram.ap(), arena[0:HEADS, R4 + 1152:R4 + 1152 + LINE + 1]).then_inc(line_stored, 16)

            after_phase(sp, "attn_norm")
            wq = t["w_qkv"][0].rearrange("(k p) n -> p k n", p=P)
            for n in range(6):
                if n >= 2:
                    sp.wait_ge(qkv_mm, NT * (n - 1))
                sp.dma_start(wqkv_ring[n % 2], wq[:, :, BANK * n:BANK * (n + 1)]).then_inc(wqkv_in[n % 2], 16)

            after_phase(sp, "qkv")
            sp.wait_ge(line_stored, 16)
            sp.dma_start(strip_flipped, bass.AP(tensor=line_dram, offset=0, ap=[[1, P], [LINE + 1, HEADS], [1, 2 * P]])
                         ).then_inc(strip_in, 16)
            sp.wait_ge(strip_turned, 1)
            sp.dma_start(wo, t["w_o"][0].rearrange("(k p) n -> p k n", p=P)).then_inc(wo_in, 16)

            def moe(l, before):
                m, once = moe_of[l], l + 1
                after_phase(sp, before)

                def load_weights(e, b, k):
                    src = (t["w_gate"], t["w_up"], t["w_down"])[k][l]
                    src = src[ds(e, 1)].rearrange("a (k p) n -> p (a k) n", p=P) if not isinstance(e, int) else \
                        src[e].rearrange("(k p) n -> p k n", p=P)
                    sp.dma_start(wslot[b][k], src).then_inc(w_in_sem[k][b], 16)

                sp.dma_start(w_router[:, :, 0:GROUPS], t["router_group_w"][l].rearrange("(k p) n -> p k n", p=P)
                             ).then_inc(router_in, 16)
                sp.dma_start(w_router[:, :, GROUPS:], t["router_expert_w"][l].rearrange("(k p) n -> p k n", p=P)
                             ).then_inc(router_in, 16)
                sp.dma_start(b_router[:, 0:GROUPS], row_of(t["router_group_b"], GROUPS, l * GROUPS)
                             ).then_inc(router_in, 16)
                sp.dma_start(b_router[:, GROUPS:], row_of(t["router_expert_b"], NE, l * NE)).then_inc(router_in, 16)
                sp.wait_ge(clear_ready, once)
                sp.dma_start(slots_dram[l].ap().rearrange("(p a) b -> p (a b)", p=P), no_slots
                             ).then_inc(table_cleared, 16)
                for e in range(2):
                    for k in range(3):
                        load_weights(e, e, k)
                rows = normed_dram[l].rearrange("(t p) d -> p t d", p=P)
                n0 = PAIRS * NORMS.index(f"ffn{l}")
                with sp.Fori(0, NT // 2) as ip:
                    for b in range(2):
                        sp.wait_ge(norm_rows_ready[b], n0 + ip + 1)
                        sp.dma_start(rows[:, ds(2 * ip + b, 1), :], normed[b].unsqueeze(1)).then_inc(stored[b], 16)
                sp.wait_ge(masks, once)
                for b in range(2):
                    sp.wait_ge(stored[b], 16 * PAIRS * once + 16)
                for k in range(3):
                    load_weights(2, 2, k)
                sp.wait_ge(tabled, 16 * 2 * NT * once)
                sp.dma_start(slot_all, slots_dram[l].ap().rearrange("(j p e) b -> p j (e b)", p=P, e=NE)
                             ).then_inc(table_in, 16)
                sp.wait_ge(lists, once)

                def next_expert(e, b, turn_of_slot):
                    first = [NE // RING * l + (l if j < NE % RING else 0) for j in range(RING)]
                    before, prev = (b - 1) % RING, turn_of_slot - (b == 0)
                    in_flight = [(before, 1, prev), (before, 2, prev), (b, 0, turn_of_slot)]
                    tiles_through = sp.value_load(meta[0:1, ds(e - 2, 1), 1:2], min_val=1, max_val=64)
                    products_through = sp.to_reg(tiles_through * KF)
                    landed = [sp.to_reg(16 * (first[slot] + turn_ + 1)) for slot, _, turn_ in in_flight]
                    for k in range(3):
                        slot, kind, _ = in_flight[k]
                        sp.wait_ge(w_in_sem[kind][slot], landed[k])
                        if k == 0:
                            sp.wait_ge(m.gate_up, products_through)
                        if k == 2:
                            sp.wait_ge(m.down, tiles_through)
                        load_weights(e, b, k)

                with sp.Fori(1, NE // RING) as er:
                    for b in range(RING):
                        next_expert(er * RING + b, b, er)
                for b in range(NE % RING):
                    next_expert(NE // RING * RING + b, b, NE // RING)
                tiles = sp.value_load(total[0:1, 0:1], min_val=1, max_val=64)
                sp.wait_ge(m.scattered, tiles * 16 + 32)
                pairs = expert_out_dram[l].rearrange("(t p k) d -> p t k d", p=P, k=2)
                for i in range(NT):
                    b = i % 2
                    if i >= 2:
                        sp.wait_ge(pair_used[b], PAIRS * l + i // 2)
                    sp.dma_start(y_pair[b], pairs[:, i]).then_inc(pair_in[b], 16)
                    if l == 1 and i >= 1:
                        store_out(i - 1)
                if l == 1:
                    store_out(NT - 1)

            def store_out(i):
                sp.wait_ge(pair_used[i % 2], PAIRS + i // 2 + 1)
                sp.dma_start(out[0].rearrange("(t p) d -> p t d", p=P)[:, i, :], x[:, i, :]).then_inc(out_stored, 16)

            moe(0, "projection")

            after_phase(sp, "moe0")
            sp.dma_start(w_in, t["pool_w_in"][0].rearrange("(k p) n -> p k n", p=P)).then_inc(pool_in, 16)
            sp.dma_start(w_grp, t["pool_w_group"][0].rearrange("g (k p) n -> p (g k) n", p=P)).then_inc(pool_in, 16)
            sp.dma_start(w_out, t["pool_w_out"][0].rearrange("(k p) n -> p k n", p=P)).then_inc(pool_in, 16)
            sp.dma_start(scale_row, row_of(t["pool_scale"], D)).then_inc(pool_in, 16)

            moe(1, "pool")
            sp.wait_ge(out_stored, 16 * NT)

        def norm_act(act, name):
            with act.Fori(0, NT) as i:
                act.wait_ge(norm_ssq, NT * NORMS.index(name) + i + 1)
                nc.scalar.activation(square, x[:, ds(i, 1), :].rearrange("p a d -> p (a d)"), ACT.Square,
                                     accum_out=ssq[:, ds(i, 1)]).then_inc(norm_ssq, 1)
            act.wait_ge(norm_ssq, NT * (NORMS.index(name) + 1) + 1)
            nc.scalar.activation(std, ssq, ACT.Sqrt, bias=eps_t, scale=1.0 / D).then_inc(norm_std, 1)

        def norm_rows(ip, b):
            nc.vector.tensor_scalar(normed[b], x[:, ds(2 * ip + b, 1), :].rearrange("p a d -> p (a d)"),
                                    rstd[:, ds(2 * ip + b, 1)], None, ALU.mult).then_inc(norm_rows_ready[b], 1)

        def turn(src, dst_bank, n, done):
            for k in range(n):
                last = nc.tensor.transpose(psum[:, BANK * dst_bank + P * k:BANK * dst_bank + P * (k + 1)],
                                           src(k), ident)
            last.then_inc(done, 1)

        @block.tensor
        def _(pe):
            pe.wait_ge(params_in, 16 * N_PARAMS)
            pe.wait_ge(rel_in, 16)
            pe.wait_ge(rel_zeroed, 3)
            nc.tensor.matmul(psum[:, 0:LINE + 1], arena[:, R4 + 1024:R4 + 1152], view(R4 + 512, LINE + 1),
                             start=True, stop=True).then_inc(line_psum, 1)
            end_phase(pe, "setup")

            def norm_turn(name):
                n0 = PAIRS * NORMS.index(name)
                with pe.Fori(0, NT // 2) as ip:
                    for b in range(2):
                        pe.wait_ge(norm_rows_ready[b], n0 + ip + 1)
                        pe.wait_ge(norm_kept[b], n0 + ip + 1)
                        turn(lambda k: normed[b][:, P * k:P * (k + 1)], 2 * b, KD, norm_turned[b])

            norm_turn("attn")
            end_phase(pe, "attn_norm")

            def qkv_unit(ch, i, u, clear):
                pe.wait_ge(*clear)
                for k in range(KD):
                    last = nc.tensor.matmul(bank(i % 2), hT[:, k, P * i:P * (i + 1)], wqkv_ring[ch][:, k, :],
                                            start=k == 0, stop=k == KD - 1)
                last.then_inc(qkv_mm, 1)
                return last

            def qk_turn(i, u):
                pe.wait_ge(qk_ready, u + 1 + 1)
                if i >= 0:
                    turn(lambda k: qk_rows[i % 2].rearrange("p a b -> p (a b)")[:, P * k:P * (k + 1)],
                         4 + i % 2, 4, qk_turned)

            with pe.Fori(0, 2) as np_:
                for s in range(2):
                    pe.wait_ge(wqkv_in[s], 16 * np_ + 16)
                    for i in range(NT):
                        u = 16 * np_ + 8 * s + i
                        if i < 2:
                            pe.wait_ge(qk_ready, 16 * np_ + 8 * s + 1)
                        else:
                            pe.wait_ge(qk_ready, u - 1 + 1)
                        for k in range(KD):
                            last = nc.tensor.matmul(bank(i % 2), hT[:, k, P * i:P * (i + 1)], wqkv_ring[s][:, k, :],
                                                    start=k == 0, stop=k == KD - 1)
                        last.then_inc(qkv_mm, 1)
                        if i >= 1:
                            qk_turn(i - 1, u - 1)
                    qk_turn(NT - 1, 16 * np_ + 8 * s + NT - 1)
            for s in range(2):
                pe.wait_ge(wqkv_in[s], 16 * 3)
                for i in range(NT):
                    uv = 8 * s + i
                    if uv >= 2:
                        pe.wait_ge(v_kept, uv - 1)
                    for k in range(KD):
                        last = nc.tensor.matmul(bank(i % 2), hT[:, k, P * i:P * (i + 1)], wqkv_ring[s][:, k, :],
                                                start=k == 0, stop=k == KD - 1)
                    last.then_inc(qkv_mm, 1)
            end_phase(pe, "qkv")

            score_bank, turn_bank, av_bank = (0, 2), 4, (6, 7)

            pe.wait_ge(strip_in, 16)
            for n in range(4):
                last = nc.tensor.matmul(bank(n), const[:, C_FLIP:], strip_flipped[:, 2 * n:2 * n + 2, :],
                                        start=True, stop=True)
            last.then_inc(strip_turned, 1)

            def att_scores(hp, s, qb, first_use):
                st = 16 * hp + 8 * s + qb
                if qb == 0:
                    pe.wait_ge(staged[s], 2 * hp + 2)
                for c in range(2):
                    if not first_use:
                        pe.wait_ge(exped[c], st)
                    width = P * (qb + 1)
                    for w0 in range(0, width, BANK):
                        w = min(BANK, width - w0)
                        last = nc.tensor.matmul(psum[:, BANK * score_bank[c] + w0:BANK * score_bank[c] + w0 + w],
                                                q_head[s][HD * c:HD * (c + 1), P * qb:P * (qb + 1)],
                                                k_head[s][HD * c:HD * (c + 1), w0:w0 + w], start=True, stop=True)
                    last.then_inc(scores[c], 1)

            def att_av(h, qb, st, par, bank_used):
                pe.wait_ge(p_kept, st + 1)
                if bank_used:
                    pe.wait_ge(o_kept, st - 1)
                for kt in range(qb + 1):
                    last = nc.tensor.matmul(psum[:, BANK * av_bank[par]:BANK * av_bank[par] + P], probT[:, kt, :],
                                            v[:, kt, ds(h * P, P)] if not isinstance(h, int) else
                                            v[:, kt, P * h:P * (h + 1)],
                                            start=kt == 0, stop=kt == qb)
                last.then_inc(av_done, 1)

            def att_turn(qb, st, par, turned_before):
                pe.wait_ge(combined, st + 1)
                if turned_before:
                    pe.wait_ge(p_kept, st)
                turn(lambda k: prob0[par][:, P * k:P * (k + 1)], turn_bank, qb + 1, p_turned)

            def att_pe(hp, first):
                for k in range(16):
                    s, qb = divmod(k, 8)
                    att_scores(hp, s, qb, first and k == 0)
                    if not (first and k < 2):
                        kk = k - 2
                        h = 2 * hp + kk // 8
                        att_av(h, kk % 8, 16 * hp + kk, kk % 2, not (first and k < 4))
                    if not (first and k < 1):
                        kk = k - 1
                        att_turn(kk % 8, 16 * hp + kk, kk % 2, not (first and k < 2))

            pe.wait_ge(strip_kept, 1)
            att_pe(0, True)
            with pe.Fori(1, 4) as hp:
                att_pe(hp, False)
            att_av(7, 6, 62, 0, True)
            att_turn(7, 63, 1, True)
            att_av(7, 7, 63, 1, True)
            end_phase(pe, "attention")

            pe.wait_ge(wo_in, 16)
            with pe.Fori(0, NT // 2) as ip:
                for b in range(2):
                    pe.wait_ge(on_ready[b], ip + 1)
                    pe.wait_ge(oT_kept[b], ip + 1)
                    turn(lambda k: o_normed[b][:, k, :], 4 + 2 * b, KD, o_turned[b])
                for b in range(2):
                    pe.wait_ge(oT_kept[b], ip + 1 + 1)
                    pe.wait_ge(proj_added[b], ip + 1)
                    for half in range(2):
                        for k in range(KD):
                            last = nc.tensor.matmul(bank(2 * b + half), oT[b][:, k, :],
                                                    wo[:, k, BANK * half:BANK * (half + 1)],
                                                    start=k == 0, stop=k == KD - 1)
                    last.then_inc(proj_mm[b], 1)
            end_phase(pe, "projection")

            def moe(l):
                m, name = moe_of[l], f"ffn{l}"
                n0, once = PAIRS * NORMS.index(name), l + 1
                pe.wait_ge(router_in, 64 * once)
                with pe.Fori(0, NT // 2) as ip:
                    for b in range(2):
                        pe.wait_ge(norm_rows_ready[b], n0 + ip + 1)
                        pe.wait_ge(norm_kept[b], n0 + ip + 1)
                        turn(lambda k: normed[b][:, P * k:P * (k + 1)], 2 * b, KD, norm_turned[b])
                    for b in range(2):
                        pe.wait_ge(norm_kept[b], n0 + ip + 1 + 1)
                        pe.wait_ge(biased[b], PAIRS * l + ip + 1)
                        for k in range(KD):
                            last = nc.tensor.matmul(psum[:, BANK * (4 + b):BANK * (4 + b) + GROUPS + NE],
                                                    rT[b][:, k, :], w_router[:, k, :],
                                                    start=k == 0, stop=k == KD - 1)
                        last.then_inc(logits[b], 1)
                pe.wait_ge(masks, once)
                nc.tensor.matmul(psum[:, 3072:3072 + 256], tri, t256[3].rearrange("p a b -> p (a b)"),
                                 start=True, stop=True)
                nc.tensor.matmul(psum[:, 3584:3584 + 256], ones[:], t256[3].rearrange("p a b -> p (a b)"),
                                 start=True, stop=True).then_inc(ranks, 1)

                GATE, UP, TURN, DOWN = 0, 2, 4, 6

                def turn_rows(g1):
                    pe.wait_ge(m.rows_in, 16 * g1)
                    turn(lambda k: x_rows[:, P * k:P * (k + 1)], TURN, KD, m.turned)

                pe.wait_ge(lists, once)
                turn_rows(1)

                def expert(e, b, turn_of_slot):
                    wg, wu, wd = wslot[b]
                    loaded = NE // RING * l + (l if b < NE % RING else 0) + turn_of_slot + 1
                    tiles = pe.value_load(meta[0:1, ds(e, 1), 0:1], min_val=1, max_val=8)
                    before = pe.value_load(meta[0:1, ds(e, 1), 1:2], min_val=0, max_val=64)
                    tokens = pe.value_load(meta[0:1, ds(e, 1), 2:3], min_val=0, max_val=S)
                    with pe.Fori(0, tiles) as j:
                        g = before + j
                        for k in range(2):
                            pe.wait_ge(w_in_sem[k][b], 16 * loaded)
                        pe.wait_ge(m.xT_kept, g + 1)

                        def gate_up(n):
                            for f in range(KF):
                                if f >= 2:
                                    pe.wait_ge(m.hidden, KF * g + f - 1)
                                for w, at in ((wg, GATE + f % 2), (wu, UP + f % 2)):
                                    for k in range(KD):
                                        last = nc.tensor.matmul(psum[:, BANK * at:BANK * at + n],
                                                                w[:, k, P * f:P * (f + 1)], xT[:, k, 0:n],
                                                                start=k == 0, stop=k == KD - 1)
                                last.then_inc(m.gate_up, 1)

                        with pe.If(tokens - j * P <= 64):
                            gate_up(64)
                        with pe.Else():
                            with pe.If(tokens - j * P <= 96):
                                gate_up(96)
                            with pe.Else():
                                gate_up(P)
                        turn_rows(g + 2)
                        pe.wait_ge(w_in_sem[2][b], 16 * loaded)
                        pe.wait_ge(m.hidden, KF * g + KF)
                        pe.wait_ge(m.y_kept, 2 * g + 1)
                        for half in range(2):
                            for f in range(KF):
                                last = nc.tensor.matmul(bank(DOWN + half), hiddenT[:, f, :],
                                                        wd[:, f, BANK * half:BANK * (half + 1)],
                                                        start=f == 0, stop=f == KF - 1)
                        last.then_inc(m.down, 1)

                with pe.Fori(0, NE // RING) as er:
                    for b in range(RING):
                        expert(er * RING + b, b, er)
                for b in range(NE % RING):
                    expert(NE // RING * RING + b, b, NE // RING)
                end_phase(pe, f"moe{l}")

            moe(0)

            norm_turn("pool")
            end_phase(pe, "pool_norm")
            pe.wait_ge(pool_in, 64)
            n = 0
            for c in range(KD):
                for half in range(2):
                    if n >= 2:
                        pe.wait_ge(u_kept, n - 1)
                    for k in range(KD):
                        last = nc.tensor.matmul(bank(n % 2), w_in[:, k, P * c:P * (c + 1)],
                                                hT[:, k, BANK * half:BANK * (half + 1)],
                                                start=k == 0, stop=k == KD - 1)
                    last.then_inc(u_mm, 1)
                    n += 1
            n = 0
            for g in range(len(WINDOWS)):
                pe.wait_ge(pooled, 2 * g + 2)
                for ec in range(2):
                    for half in range(2):
                        if n >= 2:
                            pe.wait_ge(mix_kept, n - 1)
                        for kc in range(2):
                            last = nc.tensor.matmul(bank(2 + n % 2), w_grp[:, 2 * g + kc, P * ec:P * (ec + 1)],
                                                    uT[:, 2 * g + kc, PAD + BANK * half:PAD + BANK * (half + 1)],
                                                    start=kc == 0, stop=kc == 1)
                        last.then_inc(mix_mm, 1)
                        n += 1
            pe.wait_ge(mix_kept, 16)
            for i in range(NT):
                if i >= 2:
                    pe.wait_ge(out_added, i - 1)
                for half in range(2):
                    for k in range(KD):
                        last = nc.tensor.matmul(bank(4 + 2 * (i % 2) + half), mixedT[:, k, P * i:P * (i + 1)],
                                                w_out[:, k, BANK * half:BANK * (half + 1)],
                                                start=k == 0, stop=k == KD - 1)
                last.then_inc(out_mm, 1)
            end_phase(pe, "pool")
            moe(1)

        @block.scalar
        def _(act):
            act.wait_ge(lam_sums, 1)
            nc.scalar.activation(lam_t[:, 2:4], lam_t[:, 0:2], ACT.Exp).then_inc(lam_exp, 1)
            end_phase(act, "setup")
            act.wait_ge(x_in, 16)
            norm_act(act, "attn")
            end_phase(act, "attn_norm")

            with act.Fori(0, 2) as np_:
                for k in range(16):
                    u = 16 * np_ + k
                    act.wait_ge(qkv_mm, u + 1)
                    act.wait_ge(qk_ssq, u + 1)
                    nc.scalar.activation(qk_square.rearrange("p a b -> p (a b)"), bank(k % 2), ACT.Square
                                         ).then_inc(qk_sq, 1)
                    act.wait_ge(qk_ssq, u + 1 + 1)
                    nc.scalar.activation(std, ssq, ACT.Sqrt, bias=eps_t, scale=1.0 / HD).then_inc(qk_std, 1)
            for n in range(16):
                act.wait_ge(qkv_mm, 32 + n + 1)
                nc.scalar.activation(v[:, n % 8, BANK * (n // 8):BANK * (n // 8 + 1)], bank(n % 2), ACT.Copy
                                     ).then_inc(v_kept, 1)
            end_phase(act, "qkv")

            def att_exp(hp, k, c, first):
                st, par, width = 16 * hp + k, k % 2, P * (k % 8 + 1)
                act.wait_ge(maxed[c], st + 1)
                if not (first and k < 2) and c == 0:
                    act.wait_ge(p_turned, st - 1)
                if not (first and k < 1) and c == 1:
                    act.wait_ge(combined, st)
                nc.scalar.activation((prob0[par] if c == 0 else prob1)[:, 0:width],
                                     psum[:, BANK * 2 * c:BANK * 2 * c + width], ACT.Exp,
                                     bias=neg_max[:, par, c:c + 1], accum_out=sums[:, par, c:c + 1]
                                     ).then_inc(exped[c], 1)

            def att_keep(st, qb, first):
                act.wait_ge(p_turned, st + 1)
                if not first:
                    act.wait_ge(av_done, st)
                nc.scalar.activation(probT[:, 0:qb + 1, :].rearrange("p a b -> p (a b)"),
                                     psum[:, BANK * 4:BANK * 4 + P * (qb + 1)], ACT.Copy).then_inc(p_kept, 1)

            def att_act(hp, first):
                for k in range(16):
                    for c in range(2):
                        att_exp(hp, k, c, first)
                    if not (first and k < 1):
                        att_keep(16 * hp + k - 1, (k - 1) % 8, first and k < 2)

            att_act(0, True)
            with act.Fori(1, 4) as hp:
                att_act(hp, False)
            att_keep(63, 7, False)
            end_phase(act, "attention")

            with act.Fori(0, NT // 2) as ip:
                for b in range(2):
                    i = 2 * ip + b
                    act.wait_ge(o_ssq, i + 1)
                    nc.scalar.activation(o_square, o_rows[:, :, ds(i * P, P)], ACT.Square).then_inc(o_sq, 1)
                    act.wait_ge(o_ssq, i + 1 + 1)
                    nc.scalar.activation(std, ssq, ACT.Sqrt, bias=eps_t, scale=1.0 / P).then_inc(o_std, 1)
            end_phase(act, "projection")

            def moe(l):
                m, once = moe_of[l], l + 1
                norm_act(act, f"ffn{l}")
                act.wait_ge(act_in, 2 * l + 1)
                nc.scalar.activation(t32[1].rearrange("p a b -> p (a b)"), t32[0].rearrange("p a b -> p (a b)"),
                                     ACT.Exp).then_inc(act_out, 1)
                act.wait_ge(act_in, 2 * l + 2)
                nc.scalar.activation(t8[:, 7, :], t8[:, 6, :], ACT.Exp).then_inc(act_out, 1)
                act.wait_ge(lists, once)
                tiles = act.value_load(total[0:1, 0:1], min_val=1, max_val=64)
                with act.Fori(0, tiles) as g:
                    for f in range(KF):
                        act.wait_ge(m.gate_up, KF * g + f + 1)
                        nc.scalar.activation(gated[:, f, :], bank(f % 2)[:, 0:P], ACT.Silu).then_inc(m.silu, 1)
                    act.wait_ge(m.down, g + 1)
                    act.wait_ge(m.scattered, 16 * g + 32)
                    nc.scalar.activation(y_rows[:, 0:BANK], bank(6), ACT.Copy).then_inc(m.y_kept, 1)
                end_phase(act, f"moe{l}")

            moe(0)
            norm_act(act, "pool")
            end_phase(act, "pool_norm")
            act.wait_ge(pads, 1)
            for n in range(2 * KD):
                c, half = divmod(n, 2)
                act.wait_ge(u_mm, n + 1)
                nc.scalar.activation(uT[:, c, PAD + BANK * half:PAD + BANK * (half + 1)], bank(n % 2), ACT.Copy
                                     ).then_inc(u_kept, 1)
            for n in range(16):
                c, half = divmod(n, 2)
                act.wait_ge(mix_mm, n + 1)
                nc.scalar.activation(mixedT[:, c, BANK * half:BANK * (half + 1)], bank(2 + n % 2), ACT.Copy
                                     ).then_inc(mix_kept, 1)
            end_phase(act, "pool")
            moe(1)

        @block.vector
        def _(dve):
            link = Link(dve, dve_link)
            nc.vector.memset(arena[:, R4 + 1024:R4 + 1152], 0.0).then_inc(rel_zeroed, 1)
            dve.wait_ge(rel_zeroed, 1)
            nc.vector.memset(arena[BUCKETS:BUCKETS + 1, R4 + 1024:R4 + 1024 + HEADS], MASKED).then_inc(rel_zeroed, 1)
            nc.vector.memset(eps_t, EPS)
            nc.vector.memset(ones[:], 1.0).then_inc(rel_zeroed, 1)
            dve.wait_ge(params_in, 16 * N_PARAMS)
            lq = [view(R4 + 64 * j, HD) for j in range(4)]
            link(nc.vector.tensor_tensor(out=view(R4 + 256, HD), in0=lq[0], in1=lq[1], op=ALU.mult))
            link(nc.vector.tensor_tensor(out=view(R4 + 320, HD), in0=lq[2], in1=lq[3], op=ALU.mult))
            nc.vector.tensor_reduce(out=lam_t[:, 0:2], in_=view(R4 + 256, 2, HD), axis=AX.X, op=ALU.add
                                    ).then_inc(lam_sums, 1)
            nc.vector.tensor_scalar(qk_gain[:, 0:2], qk_gain[:, 0:2], HD ** -0.5, None, ALU.mult)
            nc.vector.tensor_scalar(sub_gain[:], sub_gain[:], 1.0 - LAMBDA_INIT, None, ALU.mult)
            dve.wait_ge(lam_exp, 1)
            link(nc.vector.tensor_tensor(out=lam_t[:, 4:5], in0=lam_t[:, 3:4], in1=lam_t[:, 2:3], op=ALU.subtract))
            link(nc.vector.tensor_scalar(neg_lam, lam_t[:, 4:5], -LAMBDA_INIT, None, ALU.add))
            dve.wait_ge(line_psum, 1)
            nc.vector.tensor_copy(arena[0:HEADS, R4 + 1152:R4 + 1152 + LINE + 1], psum[0:HEADS, 0:LINE + 1]
                                  ).then_inc(line_sb, 1)
            dve.wait_ge(line_stored, 16)
            end_phase(dve, "setup")

            def norm_rstd(name):
                dve.wait_ge(norm_std, NORMS.index(name) + 1)
                link(nc.vector.reciprocal(rstd, std))

            def keep_turned(b, dst, gain):
                nc.vector.tensor_tensor(out=dst, in0=bank(2 * b, 2).rearrange("p (k q) -> p k q", k=KD),
                                        in1=gain.unsqueeze(2).to_broadcast([P, KD, P]), op=ALU.mult
                                        ).then_inc(norm_kept[b], 1)

            def norm_dve(name, gain):
                n0 = PAIRS * NORMS.index(name)
                norm_rstd(name)
                with dve.Fori(0, NT // 2) as ip:
                    for b in range(2):
                        dve.wait_ge(norm_turned[b], n0 + ip + 1)
                        norm_rows(ip, b)
                    for b in range(2):
                        dve.wait_ge(norm_turned[b], n0 + ip + 1 + 1)
                        keep_turned(b, hT[:, :, ds((2 * ip + b) * P, P)], gain)

            norm_dve("attn", gains[:, 0, :])
            end_phase(dve, "attn_norm")

            with dve.Fori(0, 2) as np_:
                chunk_link = Link(dve, qk_link, np_ * 16)
                for k in range(16):
                    u = 16 * np_ + k
                    dve.wait_ge(qk_sq, u + 1)
                    nc.vector.tensor_reduce(out=ssq, in_=qk_square, axis=AX.X, op=ALU.add).then_inc(qk_ssq, 1)
                    dve.wait_ge(qk_std, u + 1)
                    chunk_link(nc.vector.reciprocal(rstd, std))
                    nc.vector.tensor_tensor(out=qk_rows[k % 2], in0=bank(k % 2).rearrange("p (a b) -> p a b", a=8),
                                            in1=rstd.unsqueeze(2).to_broadcast([P, 8, HD]), op=ALU.mult
                                            ).then_inc(qk_ready, 1)
                    dve.wait_ge(qk_turned, u + 1)
                    n = 2 * np_ + k // 8
                    nc.vector.tensor_scalar(qkT[:, ds(n * 4, 4), P * (k % 8):P * (k % 8 + 1)],
                                            bank(4 + k % 2).rearrange("p (a b) -> p a b", a=4),
                                            qk_gain[:, ds(n, 1)], None, ALU.mult).then_inc(qk_kept, 1)
            end_phase(dve, "qkv")

            dve.wait_ge(strip_turned, 1)
            nc.vector.tensor_copy(strip, bank(0, 4).rearrange("p (h k) -> p h k", h=HEADS)).then_inc(strip_kept, 1)
            dve.wait_ge(strip_kept, 1)

            def att_prep(hp, k, c, al):
                st, s, qb = 16 * hp + k, k // 8, k % 8
                near = P * min(qb + 1, 2)
                end = BANK * 2 * c + P * (qb + 1)
                dve.wait_ge(scores[c], st + 1)
                h = 2 * hp + s
                al(nc.vector.tensor_tensor(out=psum[:, end - near:end], in0=psum[:, end - near:end],
                                           in1=(strip[:, h, 2 * P - near:] if isinstance(h, int) else
                                                strip[:, ds(h, 1), 2 * P - near:].rearrange("p a b -> p (a b)")),
                                           op=ALU.add))
                nc.vector.tensor_reduce(out=neg_max[:, k % 2, c:c + 1], in_=psum[:, BANK * 2 * c:end], axis=AX.X,
                                        op=ALU.max, negate=True).then_inc(maxed[c], 1)

            def att_combine(st, par, qb, al):
                for c in range(2):
                    dve.wait_ge(exped[c], st + 1)
                al(nc.vector.reciprocal(rsum[:, par, :], sums[:, par, :]))
                al(nc.vector.tensor_scalar(coef[:, par:par + 1], sums[:, par, 0:1], rsum[:, par, 1:2], neg_lam,
                                           ALU.mult, ALU.mult))
                w = P * (qb + 1)
                nc.vector.scalar_tensor_tensor(out=prob0[par][:, 0:w], in0=prob1[:, 0:w], scalar=coef[:, par:par + 1],
                                               in1=prob0[par][:, 0:w], op0=ALU.mult, op1=ALU.add
                                               ).then_inc(combined, 1)

            def att_out(h, st, par, qb):
                dve.wait_ge(av_done, st + 1)
                dst = (o_rows[:, h, P * qb:P * (qb + 1)] if isinstance(h, int) else
                       o_rows[:, ds(h, 1), P * qb:P * (qb + 1)].rearrange("p a b -> p (a b)"))
                nc.vector.tensor_scalar(dst, psum[:, BANK * (6 + par):BANK * (6 + par) + P], rsum[:, par, 0:1], None,
                                        ALU.mult).then_inc(o_kept, 1)

            def att_dve(hp, first, al):
                for k in range(16):
                    att_prep(hp, k, 0, al)
                    if not (first and k < 1):
                        att_combine(16 * hp + k - 1, (k - 1) % 2, (k - 1) % 8, al)
                    att_prep(hp, k, 1, al)
                    if not (first and k < 2):
                        kk = k - 2
                        att_out(2 * hp + kk // 8, 16 * hp + kk, kk % 2, kk % 8)

            al = Link(dve, att_link)
            att_dve(0, True, al)
            assert al.n == 16 * 4 - 2
            with dve.Fori(1, 4) as hp:
                al = Link(dve, att_link, hp * 64 - 2)
                att_dve(hp, False, al)
                assert al.n == 64
            al = Link(dve, att_link, 4 * 64 - 2)
            att_out(7, 62, 0, 6)
            dve.wait_ge(o_kept, 63)
            att_combine(63, 1, 7, al)
            att_out(7, 63, 1, 7)
            end_phase(dve, "attention")

            with dve.Fori(0, NT // 2) as ip:
                ol = Link(dve, o_link, ip * 2)
                for b in range(2):
                    i = 2 * ip + b
                    dve.wait_ge(o_sq, i + 1)
                    nc.vector.tensor_reduce(out=ssq, in_=o_square, axis=AX.X, op=ALU.add).then_inc(o_ssq, 1)
                    dve.wait_ge(o_std, i + 1)
                    ol(nc.vector.reciprocal(rstd, std))
                    nc.vector.tensor_tensor(out=o_normed[b], in0=o_rows[:, :, ds(i * P, P)],
                                            in1=rstd.unsqueeze(2).to_broadcast([P, HEADS, P]), op=ALU.mult
                                            ).then_inc(on_ready[b], 1)
                for b in range(2):
                    dve.wait_ge(o_turned[b], ip + 1)
                    nc.vector.tensor_scalar(oT[b].rearrange("p a b -> p (a b)"), bank(4 + 2 * b, 2), sub_gain[:, 0:1],
                                            None, ALU.mult).then_inc(oT_kept[b], 1)
                for b in range(2):
                    i = 2 * ip + b
                    dve.wait_ge(proj_mm[b], ip + 1)
                    xi = x[:, ds(i, 1), :].rearrange("p a d -> p (a d)")
                    nc.vector.tensor_tensor(out=xi, in0=bank(2 * b, 2), in1=xi, op=ALU.add).then_inc(proj_added[b], 1)
            end_phase(dve, "projection")

            def moe(l):
                m, name = moe_of[l], f"ffn{l}"
                n0, once = PAIRS * NORMS.index(name), l + 1
                gain = gains[:, 2 + l, :]
                nc.vector.memset(no_slots, NO_SLOT).then_inc(clear_ready, 1)
                dve.wait_ge(router_in, 64 * once)
                norm_rstd(name)
                with dve.Fori(0, NT // 2) as ip:
                    for b in range(2):
                        dve.wait_ge(norm_turned[b], n0 + ip + 1)
                        dve.wait_ge(stored[b], 16 * (PAIRS * l + ip) + 16)
                        norm_rows(ip, b)
                    for b in range(2):
                        dve.wait_ge(norm_turned[b], n0 + ip + 1 + 1)
                        keep_turned(b, rT[b], gain)
                    for b in range(2):
                        dve.wait_ge(logits[b], PAIRS * l + ip + 1)
                        nc.vector.tensor_tensor(out=logit[:, ds(2 * ip + b, 1), :].rearrange("p a b -> p (a b)"),
                                                in0=psum[:, BANK * (4 + b):BANK * (4 + b) + GROUPS + NE],
                                                in1=b_router, op=ALU.add).then_inc(biased[b], 1)
                for b in range(2):
                    dve.wait_ge(biased[b], PAIRS * once + 1)

                r = link
                iota4 = const[:, C_IOTA4:C_IOTA4 + GROUPS].unsqueeze(1).to_broadcast([P, NT, GROUPS])
                iota32 = const[:, C_IOTA32:C_IOTA32 + NE].unsqueeze(1).to_broadcast([P, NT, NE])
                grp, exp_l = logit[:, :, 0:GROUPS], logit[:, :, GROUPS:]
                gmax, gsum, gp, gi, v1, v2, dv, ed, i1, i2, ta, tb = (t8[:, j, :] for j in range(12))

                def over(a, n):
                    return a.unsqueeze(2).to_broadcast([P, NT, n])

                def tt(o, a, b, op):
                    r(nc.vector.tensor_tensor(out=o, in0=a, in1=b, op=op))

                def red(o, a, op):
                    r(nc.vector.tensor_reduce(out=o, in_=a, axis=AX.X, op=op))

                red(gmax, grp, ALU.max)
                nc.vector.tensor_tensor(out=t32[0], in0=grp, in1=over(gmax, GROUPS), op=ALU.subtract
                                        ).then_inc(act_in, 1)
                dve.wait_ge(act_out, 2 * l + 1)
                red(gsum, t32[1], ALU.add)
                r(nc.vector.reciprocal(gp, gsum))
                tt(t32[2], grp, over(gmax, GROUPS), ALU.is_equal)
                tt(t32[3], t32[2], iota4, ALU.mult)
                red(gi, t32[3], ALU.min)
                tt(t32[2], iota4, over(gi, GROUPS), ALU.is_equal)
                r(nc.vector.tensor_scalar(t32[3], t32[2], BIG, -BIG, ALU.mult, ALU.add))
                el = t256[0]
                tt(el.rearrange("p t (g e) -> p t g e", g=GROUPS), exp_l.rearrange("p t (g e) -> p t g e", g=GROUPS),
                   t32[3].unsqueeze(3).to_broadcast([P, NT, GROUPS, PER_GROUP]), ALU.add)
                one, two = t256[1], t256[2]

                def pick(vmax, idx, hot, tmp):
                    red(vmax, el, ALU.max)
                    tt(tmp, el, over(vmax, NE), ALU.is_equal)
                    tt(tmp, tmp, iota32, ALU.mult)
                    red(idx, tmp, ALU.min)
                    tt(hot, iota32, over(idx, NE), ALU.is_equal)

                pick(v1, i1, one, t256[4])
                r(nc.vector.scalar_tensor_tensor(out=el.rearrange("p a b -> p (a b)"),
                                                 in0=one.rearrange("p a b -> p (a b)"), scalar=-BIG,
                                                 in1=el.rearrange("p a b -> p (a b)"), op0=ALU.mult, op1=ALU.add))
                pick(v2, i2, two, t256[4])
                nc.vector.tensor_tensor(out=t256[3], in0=one, in1=two, op=ALU.add).then_inc(masks, 1)
                nc.vector.tensor_tensor(out=dv, in0=v2, in1=v1, op=ALU.subtract).then_inc(act_in, 1)
                dve.wait_ge(act_out, 2 * l + 2)
                r(nc.vector.tensor_scalar(ta, ed, 1.0, None, ALU.add))
                r(nc.vector.reciprocal(tb, ta))
                r(nc.vector.tensor_tensor(out=gate_w[:, :, 0], in0=tb, in1=gp, op=ALU.mult))
                r(nc.vector.tensor_tensor(out=gate_w[:, :, 1], in0=gate_w[:, :, 0], in1=ed, op=ALU.mult))
                dve.wait_ge(ranks, once)
                before, in_tile, pos = t256[4], t256[5], t256[6]
                r(nc.vector.tensor_copy(in_tile, psum[:, 3584:3584 + 256].rearrange("p (a b) -> p a b", a=NT)))
                r(nc.vector.memset(before[:, 0, :], 0.0))
                for i in range(1, NT):
                    r(nc.vector.tensor_tensor(out=before[:, i, :], in0=before[:, i - 1, :], in1=in_tile[:, i - 1, :],
                                              op=ALU.add))
                cnt, ntile, upto, tmpc = (counts[:, j, :] for j in range(4))
                r(nc.vector.tensor_tensor(out=cnt, in0=before[:, NT - 1, :], in1=in_tile[:, NT - 1, :], op=ALU.add))
                tt(pos, before, psum[:, 3072:3072 + 256].rearrange("p (a b) -> p a b", a=NT), ALU.add)
                for k, (hot, idx) in enumerate(((one, i1), (two, i2))):
                    tt(t256[5], hot, pos, ALU.mult)
                    red(ta, t256[5], ALU.add)
                    r(nc.vector.tensor_scalar(ta, ta, float(NE), IDX0, ALU.mult, ALU.add))
                    tt(tb, ta, idx, ALU.add)
                    r(nc.vector.tensor_copy(dest[:, :, k], tb))
                nc.vector.tensor_copy(dest[:, :, 1], tb).then_inc(dests, 1)
                full = t256[5].rearrange("p a b -> p (a b)")[0:1, 0:7 * NE].rearrange("p (e j) -> p e j", e=NE)
                r(nc.vector.tensor_tensor(out=full, in0=cnt[0:1].unsqueeze(2).to_broadcast([1, NE, 7]),
                                          in1=const[0:1, C_THR:C_THR + 7].unsqueeze(1).to_broadcast([1, NE, 7]),
                                          op=ALU.is_gt))
                r(nc.vector.tensor_reduce(out=ntile[0:1], in_=full, axis=AX.X, op=ALU.add))
                r(nc.vector.tensor_scalar(ntile[0:1], ntile[0:1], 1.0, None, ALU.add))
                r(nc.vector.tensor_tensor_scan(out=upto[0:1], data0=ones[0:1, 0:NE], data1=ntile[0:1], initial=0.0,
                                               op0=ALU.mult, op1=ALU.add))
                r(nc.vector.tensor_tensor(out=tmpc[0:1], in0=upto[0:1], in1=ntile[0:1], op=ALU.subtract))
                r(nc.vector.tensor_copy(meta[0:1, :, 0], ntile[0:1]))
                r(nc.vector.tensor_copy(meta[0:1, :, 1], tmpc[0:1]))
                r(nc.vector.tensor_copy(meta[0:1, :, 2], cnt[0:1]))
                r(nc.vector.tensor_copy(total[:], upto[0:1, NE - 1:NE]))
                nc.vector.memset(view(E0, 2, D), 0.0)
                dve.wait_ge(table_in, 16 * once)
                nc.vector.tensor_scalar(gather_all, slot_all, 1, None, ALU.arith_shift_right).then_inc(lists, 1)

                dve.wait_ge(lists, once)
                tiles = dve.value_load(total[0:1, 0:1], min_val=1, max_val=64)

                def keep_rows(g1):
                    dve.wait_ge(m.turned, g1 + 1)
                    nc.vector.tensor_tensor(out=xT, in0=bank(4, 2).rearrange("p (k q) -> p k q", k=KD),
                                            in1=gain.unsqueeze(2).to_broadcast([P, KD, P]), op=ALU.mult
                                            ).then_inc(m.xT_kept, 1)

                keep_rows(1)
                with dve.Fori(0, tiles) as g:
                    for f in range(KF):
                        dve.wait_ge(m.silu, KF * g + f + 1)
                        nc.vector.tensor_tensor(out=hiddenT[:, f, :], in0=gated[:, f, :],
                                                in1=bank(2 + f % 2)[:, 0:P], op=ALU.mult
                                                ).then_inc(m.hidden, 1)
                    keep_rows(g + 2)
                    dve.wait_ge(m.down, g + 1)
                    dve.wait_ge(m.scattered, 16 * g + 32)
                    nc.vector.tensor_copy(y_rows[:, BANK:], bank(7)).then_inc(m.y_kept, 1)

                for i in range(NT):
                    b = i % 2
                    dve.wait_ge(pair_in[b], 16 * (PAIRS * l + i // 2 + 1))
                    nc.vector.scalar_tensor_tensor(out=x[:, i, :], in0=y_pair[b][:, 0, :], scalar=gate_w[:, i, 0:1],
                                                   in1=x[:, i, :], op0=ALU.mult, op1=ALU.add
                                                   ).then_inc(sum_link, 1)
                    dve.wait_ge(sum_link, NT * l + i + 1)
                    nc.vector.scalar_tensor_tensor(out=x[:, i, :], in0=y_pair[b][:, 1, :], scalar=gate_w[:, i, 1:2],
                                                   in1=x[:, i, :], op0=ALU.mult, op1=ALU.add
                                                   ).then_inc(pair_used[b], 1)
                end_phase(dve, f"moe{l}")

            moe(0)
            norm_dve("pool", gains[:, 1, :])
            end_phase(dve, "pool_norm")

            for j in range(2):
                nc.vector.memset(win[j][:, 0:PAD], 0.0)
            nc.vector.memset(uT[:, :, 0:PAD], 0.0).then_inc(pads, 1)
            pl = Link(dve, pool_link)
            for c in range(KD):
                w = WINDOWS[c // 2]
                dve.wait_ge(u_kept, 2 * c + 2)
                cur, step, j = uT[:, c, :], 1, 0
                while step < w:
                    pl(nc.vector.tensor_tensor(out=win[j][:, PAD:], in0=cur[:, PAD:], in1=cur[:, PAD - step:UW - step],
                                               op=ALU.add))
                    cur, step, j = win[j], 2 * step, 1 - j
                head = small[:, 48:64]
                pl(nc.vector.tensor_tensor(out=head, in0=cur[:, PAD:2 * PAD],
                                           in1=const[:, C_CNT + PAD * (c // 2):C_CNT + PAD * (c // 2 + 1)],
                                           op=ALU.mult))
                pl(nc.vector.scalar_tensor_tensor(out=uT[:, c, 2 * PAD:], in0=cur[:, 2 * PAD:], scalar=1.0 / w,
                                                  in1=uT[:, c, 2 * PAD:], op0=ALU.mult, op1=ALU.subtract))
                nc.vector.tensor_tensor(out=uT[:, c, PAD:2 * PAD], in0=head, in1=uT[:, c, PAD:2 * PAD],
                                        op=ALU.subtract).then_inc(pooled, 1)
            for i in range(NT):
                dve.wait_ge(out_mm, i + 1)
                if i >= 1:
                    dve.wait_ge(out_added, i)
                nc.vector.tensor_tensor(out=out_scaled, in0=bank(4 + 2 * (i % 2), 2), in1=scale_row, op=ALU.mult
                                        ).then_inc(out_link, 1)
                dve.wait_ge(out_link, i + 1)
                nc.vector.tensor_tensor(out=x[:, i, :], in0=out_scaled, in1=x[:, i, :], op=ALU.add
                                        ).then_inc(out_added, 1)
            end_phase(dve, "pool")
            moe(1)

        @block.gpsimd
        def _(pool):
            last_token = pool.to_reg(S - 1)
            last_assignment = pool.to_reg(2 * S - 1)
            for s, n in CREDITS:
                pool.sem_inc(s, n)
            end_phase(pool, "setup")
            end_phase(pool, "attn_norm")
            end_phase(pool, "qkv")
            def stage_pair(hp, first):
                for s in range(2):
                    h = 2 * hp + s
                    if not first:
                        pool.wait_ge(scores[1], NT * (h - 1))
                    for dst, head in ((q_head[s], h), (k_head[s], h + HEADS)):
                        nc.gpsimd.tensor_copy(dst, qkT[:, ds(head, 1), :].rearrange("p a b -> p (a b)")
                                              ).then_inc(staged[s], 1)

            stage_pair(0, True)
            with pool.Fori(1, HEADS // 2) as hp:
                stage_pair(hp, False)
            end_phase(pool, "attention")
            end_phase(pool, "projection")

            def moe(l):
                m, once = moe_of[l], l + 1
                pool.wait_ge(dests, once)
                pool.wait_ge(table_cleared, 16 * once)
                for i in range(NT):
                    for k in range(2):
                        nc.gpsimd.indirect_dma_start(
                            out=slots_dram[l].ap(),
                            out_offset=bass.IndirectOffsetOnAxis(ap=dest[:, i, k:k + 1], axis=0),
                            in_=assignment[:, 2 * i + k:2 * i + k + 1], in_offset=None).then_inc(tabled, 16)
                pool.wait_ge(lists, once)
                for b in range(2):
                    pool.wait_ge(stored[b], 16 * PAIRS * once + 16)

                def gather(filled):
                    filled = pool.to_reg(filled)
                    pool.wait_ge(lists, once)
                    pool.wait_ge(m.pool_link, filled)
                    nc.gpsimd.indirect_dma_start(
                        out=x_rows, out_offset=None, in_=normed_dram[l],
                        in_offset=bass.IndirectOffsetOnAxis(ap=gather_now[:, 0:1], axis=0),
                        bounds_check=last_token, oob_is_err=False).then_inc(m.rows_in, 16)

                def scatter(g):
                    landed, filled, kept = pool.to_reg(16 * g + 16), pool.to_reg(3 * g + 4), pool.to_reg(2 * g + 1)
                    pool.wait_ge(lists, once)
                    pool.wait_ge(m.scattered, landed)
                    nc.gpsimd.tensor_copy(scatter_now[:], scatter_next[:]).then_inc(m.pool_link, 1)
                    pool.wait_ge(lists, once)
                    pool.wait_ge(m.pool_link, filled)
                    pool.wait_ge(m.y_kept, kept)
                    nc.gpsimd.indirect_dma_start(
                        out=expert_out_dram[l],
                        out_offset=bass.IndirectOffsetOnAxis(ap=scatter_now[:, 0:1], axis=0), in_=y_rows,
                        in_offset=None, bounds_check=last_assignment, oob_is_err=False).then_inc(m.scattered, 16)

                nc.gpsimd.tensor_copy(scatter_now[:], no_slots[:, 0:1]).then_inc(m.pool_link, 1)
                nc.gpsimd.tensor_copy(scatter_next[:], no_slots[:, 0:1]).then_inc(m.pool_link, 1)
                pool.wait_ge(m.pool_link, 2)
                nc.gpsimd.indirect_dma_start(
                    out=expert_out_dram[l], out_offset=bass.IndirectOffsetOnAxis(ap=scatter_now[:, 0:1], axis=0),
                    in_=y_rows, in_offset=None, bounds_check=last_assignment, oob_is_err=False
                    ).then_inc(m.scattered, 16)
                with pool.Fori(0, NE) as e:
                    tiles = pool.value_load(meta[0:1, ds(e, 1), 0:1], min_val=1, max_val=8)
                    before = pool.value_load(meta[0:1, ds(e, 1), 1:2], min_val=0, max_val=64)
                    with pool.Fori(0, tiles) as j:
                        g = before + j
                        pool.wait_ge(m.turned, g + 1)
                        nc.gpsimd.tensor_copy(gather_now[:], gather_all[:, ds(j, 1), ds(e, 1)].rearrange(
                            "p a b -> p (a b)")).then_inc(m.pool_link, 1)
                        gather(3 * g + 3)
                        scatter(g)
                        nc.gpsimd.tensor_copy(scatter_next[:], slot_all[:, ds(j, 1), ds(e, 1)].rearrange(
                            "p a b -> p (a b)")).then_inc(m.pool_link, 1)
                last = pool.value_load(total[0:1, 0:1], min_val=1, max_val=64)
                pool.wait_ge(m.turned, last + 1)
                gather(3 * last + 2)
                landed, filled, kept = (pool.to_reg(v) for v in (16 * last + 16, 3 * last + 3, 2 * last + 1))
                pool.wait_ge(lists, once)
                pool.wait_ge(m.scattered, landed)
                nc.gpsimd.tensor_copy(scatter_now[:], scatter_next[:]).then_inc(m.pool_link, 1)
                pool.wait_ge(lists, once)
                pool.wait_ge(m.pool_link, filled)
                pool.wait_ge(m.y_kept, kept)
                nc.gpsimd.indirect_dma_start(
                    out=expert_out_dram[l], out_offset=bass.IndirectOffsetOnAxis(ap=scatter_now[:, 0:1], axis=0),
                    in_=y_rows, in_offset=None, bounds_check=last_assignment, oob_is_err=False
                    ).then_inc(m.scattered, 16)
                end_phase(pool, f"moe{l}")

            moe(0)
            end_phase(pool, "pool_norm")
            end_phase(pool, "pool")
            moe(1)


_INS = ["x", "rel_bias", "attn_norm", "w_qkv", "q_gain", "k_gain", "lambda_q1", "lambda_k1", "lambda_q2",
        "lambda_k2", "subln_gain", "w_o", "pool_norm", "pool_w_in", "pool_w_group", "pool_w_out", "pool_scale",
        "ffn_norm", "router_group_w", "router_group_b", "router_expert_w", "router_expert_b", "w_gate", "w_up",
        "w_down"]


def kernel(**inputs):
    import numpy as _np
    import concourse.bacc as _bacc
    from concourse import mybir as _mybir
    from concourse.bass_utils import run_bass_kernel_spmd as _run

    nc = _bacc.Bacc("TRN2", target_bir_lowering=False, num_devices=1)
    arrays, aps = {}, {}
    given = {name: _np.ascontiguousarray(inputs[name]) for name in _INS}
    given["const"] = float_constants()
    given["bias_line"] = bias_line_constants()
    given["assignment"] = int_constants()
    for name, a in given.items():
        arrays[f"in_{name}"] = a
        aps[name] = nc.dram_tensor(f"in_{name}", a.shape, _mybir.dt.from_np(a.dtype), kind="ExternalInput").ap()
    out = nc.dram_tensor("out", (1, S, D), _mybir.dt.float32, kind="ExternalOutput").ap()
    hybrid_trunk_kernel(nc, aps, out)
    r = _run(nc, [arrays], core_ids=[0])
    return r.results[0]["out"]
```

```python
import math
from contextlib import ExitStack

import numpy as np

import concourse.bass as bass
from concourse import mybir

D = 1024
S = 1024
P = 128
NT = S // P
KD = D // P
HEADS = 8
HD = 64
WINDOWS = (2, 4, 8, 16)
PAD = max(WINDOWS)
GROUPS, PER_GROUP = 4, 8
NE = GROUPS * PER_GROUP
FF = D // 2
KF = FF // P
BANK = 512
EPS = 1e-6
LAMBDA_INIT = 0.8 - 0.6 * math.exp(-0.3 * 0)
BIG = 3.0e38
MASKED = -1.0e30
IDX0 = 64.0
NO_SLOT = 1 << 20
BUCKETS = 32
RING = 3
LINE = 3 * P - 1


def rel_bucket(dist):
    n = np.maximum(dist, 0)
    nf = np.maximum(n, 1).astype(np.float32)
    exact = BUCKETS // 2
    large = exact + (np.log(nf / exact) / math.log(128 / exact) * (BUCKETS - exact)).astype(np.int32)
    return np.where(n < exact, n, np.minimum(large, BUCKETS - 1))


C_IDENT, C_TRI, C_IOTA4, C_IOTA32, C_THR, C_CNT, C_FLIP = 0, 128, 256, 260, 292, 299, 363
C_END = C_FLIP + P


def float_constants():
    c = np.zeros((P, C_END), np.float32)
    c[:, C_IDENT:C_IDENT + P] = np.eye(P)
    c[:, C_TRI:C_TRI + P] = np.triu(np.ones((P, P)), 1)
    c[:, C_IOTA4:C_IOTA4 + GROUPS] = np.arange(GROUPS) - IDX0
    c[:, C_IOTA32:C_IOTA32 + NE] = np.arange(NE) - IDX0
    c[:, C_THR:C_THR + 7] = P * np.arange(1, 8)
    c[:, C_FLIP:] = np.eye(P)[::-1]
    for g, w in enumerate(WINDOWS):
        c[:, C_CNT + g * PAD:C_CNT + (g + 1) * PAD] = 1.0 / np.minimum(np.arange(1, PAD + 1), w)
    return c


def bias_line_constants():
    c = np.zeros((P, LINE + 1), np.float32)
    dist = 2 * P - 1 - np.arange(LINE)
    for m, d in enumerate(dist):
        if d >= 0:
            c[rel_bucket(np.array(d)), m] += 1.0
            c[BUCKETS - 1, m] -= 1.0
        else:
            c[BUCKETS, m] = 1.0
    return c


def int_constants():
    t = np.arange(NT)[None, :] * P + np.arange(P)[:, None]
    return (2 * t[:, :, None] + np.arange(2)).reshape(P, 2 * NT).astype(np.int32)


def hybrid_trunk_kernel(nc, t, out):
    f32, i32 = mybir.dt.float32, mybir.dt.int32
    ALU, ACT, AX = mybir.AluOpType, mybir.ActivationFunctionType, mybir.AxisListType
    ds = bass.ds
    ctx = ExitStack()
    with ctx:
        def sb(name, shape, dt=f32):
            return ctx.enter_context(nc.sbuf_tensor(name, shape, dt))

        def sem(name):
            return ctx.enter_context(nc.semaphore(name))

        def dram(name, shape, dt=f32):
            return nc.dram_tensor(name, shape, dt, kind="Internal")

        def row_of(ap, n, offset=0):
            return bass.AP(tensor=ap.tensor, offset=offset, ap=[[0, P], [1, n]])

        line_dram = dram("bias_line", (HEADS, LINE + 1))
        normed_dram = [dram(f"normed_{l}", (S, D)).ap() for l in range(2)]
        slots_dram = [dram(f"slots_{l}", (S * NE, 1), i32) for l in range(2)]
        expert_out_dram = [dram(f"expert_out_{l}", (2 * S, D)).ap() for l in range(2)]

        PAIR_BUFS = 4
        X0, R1, R2, R3, R4, END = 0, 8192, 16384, 32768, 40960, 51328
        arena = sb("arena", [P, END])

        def view(off, *dims, dt=f32):
            n = int(np.prod(dims))
            assert off + n <= END
            ap = arena[:, off:off + n]
            if dt != f32:
                ap = ap.bitcast(dt)
            if len(dims) == 2:
                ap = ap.rearrange("p (a b) -> p a b", a=dims[0])
            if len(dims) == 3:
                ap = ap.rearrange("p (a b c) -> p a b c", a=dims[0], b=dims[1])
            return ap

        x = view(X0, NT, D)
        lam_in = [view(R3 + 64 * j, HD) for j in range(4)]
        lam_prod = view(R3 + 256, 2, HD)
        line_in = view(R3 + 512, LINE + 1)
        rel = view(R3 + 1024, P)
        line = view(R3 + 1152, LINE + 1)
        hT = view(R1, KD, S)
        attn_normed = [view(R2 + 1024 * b, D) for b in range(2)]
        attn_square = view(R2 + 2048, D)
        normed = [view(R4 + 1024 * b, D) for b in range(2)]
        square = view(R4 + 2048, D)
        wqkv_ring = [view(R4 + 4096 * b, KD, BANK) for b in range(2)]
        qk_square = view(R4 + 8192, 8, HD)
        qk_rows = [view(R4 + 8704 + 512 * b, 8, HD) for b in range(2)]
        qkT = view(R2, 2 * HEADS, S)
        v = view(R3, NT, D)
        strip = view(R4, HEADS, 2 * P)
        strip_flipped = view(R4 + 8192, HEADS, 2 * P)
        q_head = [view(R4 + 2048 + 2048 * b, S) for b in range(2)]
        k_head = [view(R4 + 3072 + 2048 * b, S) for b in range(2)]
        prob0 = [view(R4 + 6144 + 1024 * b, S) for b in range(2)]
        prob1 = view(R4 + 8192, S)
        probT = view(R4 + 9216, NT, P)
        o_rows = view(R2, HEADS, S)
        wo = view(R1, KD, D)
        o_square = view(R3, HEADS, P)
        o_normed = [view(R3 + 1024 + 1024 * b, HEADS, P) for b in range(2)]
        oT = [view(R3 + 3072 + 1024 * b, KD, P) for b in range(2)]
        wslot = [(view(R1 + 12288 * b, KD, FF), view(R1 + 12288 * b + 4096, KD, FF),
                  view(R1 + 12288 * b + 8192, KF, D)) for b in range(RING)]
        E0 = R1 + 12288 * RING
        x_rows = view(E0, D)
        y_rows = view(E0 + 1024, D)
        xT = view(E0 + 2048, KD, P)
        gated = view(E0 + 3072, KF, P)
        hiddenT = view(E0 + 3584, KF, P)
        y_pair = [view(R3 + 2048 * b, 2, D) for b in range(PAIR_BUFS)]
        rT = [view(R4 + 3072 + 1024 * b, KD, P) for b in range(2)]
        t256 = [view(E0 + 256 * j, NT, NE) for j in range(7)]
        t32 = [view(E0 + 1792 + 32 * j, NT, GROUPS) for j in range(4)]
        logit = view(E0 + 1920, NT, GROUPS + NE)
        w_router = view(E0 + 2208, KD, GROUPS + NE)
        b_router = view(E0 + 2496, GROUPS + NE)
        slot_all = view(E0 + 4096, NT, NE, dt=i32)
        gather_all = view(E0 + 4352, NT, NE, dt=i32)
        no_slots = view(E0 + 4608, 256, dt=i32)
        w_in = view(R2, KD, D)
        w_out = view(R2 + 8192, KD, D)
        UW = PAD + S
        uT = view(R3, KD, UW)
        w_grp = view(R4 + 3072, KD, 2 * P)
        scale_row = view(R4 + 7168 + 2 * UW, D)
        win = [view(R4 + 6144 + UW * j, UW) for j in range(2)]
        out_scaled = view(R4 + 6144 + 2 * UW, D)
        mixedT = view(R1, KD, S)

        const = sb("const", [P, C_END])
        ident, tri = const[:, C_IDENT:C_IDENT + P], const[:, C_TRI:C_TRI + P]
        assignment = sb("assignment", [P, 2 * NT], i32)
        gains = sb("gains", [P, 4, KD])
        qk_gain = sb("qk_gain", [P, 4])
        sub_gain = sb("sub_gain", [P, 1])
        small = sb("small", [P, 88])
        eps_t = small[:, 0:1]
        neg_lam = small[:, 1:2]
        lam_t = small[:, 2:8]
        ssq, std, rstd = small[:, 8:16], small[:, 16:24], small[:, 24:32]
        neg_max = small[:, 32:36].rearrange("p (a b) -> p a b", a=2)
        sums = small[:, 36:40].rearrange("p (a b) -> p a b", a=2)
        rsum = small[:, 40:44].rearrange("p (a b) -> p a b", a=2)
        coef = small[:, 44:46]
        x_ssq, x_std, x_rstd = small[:, 64:72], small[:, 72:80], small[:, 80:88]
        ones = sb("ones", [P, P])
        t8 = sb("t8", [P, 12, NT])
        gate_w = sb("gate_w", [P, NT, 2])
        dest = sb("dest", [P, NT, 2], i32)
        counts = sb("counts", [P, 4, NE])
        meta = sb("meta", [1, NE, 4], i32)
        total = sb("total", [1, 1], i32)
        gather_now = sb("gather_now", [P, 1], i32)
        scatter_now = sb("scatter_now", [P, 1], i32)
        scatter_next = [sb(f"scatter_next{j}", [P, 1], i32) for j in range(2)]

        psum = ctx.enter_context(nc.psum_tensor("psum", [P, 8 * BANK], f32))

        def bank(b, n=1):
            return psum[:, BANK * b:BANK * (b + n)]

        phase_done = sem("phase_done")
        x_in = [sem(f"x_in{j}") for j in range(4)]
        first_params_in, params_in, rel_in = sem("first_params_in"), sem("params_in"), sem("rel_in")
        rel_zeroed, line_psum, line_sb, line_stored, strip_in = (
            sem(n) for n in ("rel_zeroed", "line_psum", "line_sb", "line_stored", "strip_in"))
        strip_turned, strip_kept = sem("strip_turned"), sem("strip_kept")
        lam_sums, lam_exp = sem("lam_sums"), sem("lam_exp")
        dve_link = sem("dve_link")

        norm_ssq, norm_std = sem("norm_ssq"), sem("norm_std")
        norm_rows_ready = [sem(f"norm_rows{b}") for b in range(2)]
        norm_turned = [sem(f"norm_turned{b}") for b in range(2)]
        norm_kept = [sem(f"norm_kept{b}") for b in range(2)]
        NORMS = ["attn", "ffn0", "pool", "ffn1"]
        PAIRS = NT // 2
        wqkv_in = [sem(f"wqkv_in{b}") for b in range(2)]
        qkv_mm, qk_sq, qk_ssq, qk_std, qk_ready, qk_turned, qk_kept, v_kept = (
            sem(n) for n in ("qkv_mm", "qk_sq", "qk_ssq", "qk_std", "qk_ready", "qk_turned", "qk_kept", "v_kept"))
        qk_link = sem("qk_link")
        staged = [sem(f"staged{b}") for b in range(2)]
        scores = [sem(f"scores{c}") for c in range(2)]
        maxed = [sem(f"maxed{c}") for c in range(2)]
        exped = [sem(f"exped{c}") for c in range(2)]
        att_link, combined, p_turned, p_kept, av_done, o_kept = (
            sem(n) for n in ("att_link", "combined", "p_turned", "p_kept", "av_done", "o_kept"))
        wo_in = sem("wo_in")
        o_sq, o_ssq, o_std, on_ready, o_turned, oT_kept = (
            sem(n) for n in ("o_sq", "o_ssq", "o_std", "on_ready", "o_turned", "oT_kept"))
        mixer_mm, mixer_scaled, mixer_added = sem("mixer_mm"), sem("mixer_scaled"), sem("mixer_added")

        router_in, table_cleared, clear_ready, act_in, act_out, masks, ranks, dests, tabled, table_in, lists = (
            sem(n) for n in ("router_in", "table_cleared", "clear_ready", "act_in", "act_out", "masks", "ranks",
                             "dests", "tabled", "table_in", "lists"))
        stored = [sem(f"stored{b}") for b in range(2)]
        logits = [sem(f"logits{b}") for b in range(2)]
        biased = [sem(f"biased{b}") for b in range(2)]
        w_in_sem = [[sem(f"w{k}_in{b}") for b in range(RING)] for k in range(3)]
        pair_in = [sem(f"pair_in{b}") for b in range(PAIR_BUFS)]
        pair_used = [sem(f"pair_used{b}") for b in range(PAIR_BUFS)]
        sum_link = sem("sum_link")

        class Moe:
            def __init__(self, l):
                def s(n):
                    return sem(f"moe{l}_{n}")
                self.pool_link = s("pool_link")
                self.rows_in, self.turned, self.xT_kept = s("rows_in"), s("turned"), s("xT_kept")
                self.gate_up, self.silu, self.hidden = s("gate_up"), s("silu"), s("hidden")
                self.down, self.y_kept, self.scattered = s("down"), s("y_kept"), s("scattered")

        moe_of = [Moe(0), Moe(1)]
        w_in_in = [sem(f"w_in_in{h}") for h in range(2)]
        pool_in, u_mm, u_kept, pooled, pool_link, mix_mm, mix_kept, pads = (
            sem(n) for n in ("pool_in", "u_mm", "u_kept", "pooled", "pool_link", "mix_mm", "mix_kept",
                             "pads"))
        out_stored = sem("out_stored")

        N_PARAMS = 18
        CREDITS = [(s, 1) for s in (qk_ssq, qk_ready)]
        for m in moe_of:
            CREDITS += [(m.y_kept, 3), (m.turned, 1)]
        PH = ["attn_norm", "qkv", "attention", "projection", "moe0", "pool", "moe1"]

        def end_phase(eng, name):
            eng.drain().then_inc(phase_done, 1)
            eng.wait_ge(phase_done, 4 * (PH.index(name) + 1))

        def after_phase(eng, name):
            eng.wait_ge(phase_done, 4 * (PH.index(name) + 1))

        class Link:
            def __init__(self, eng, s, base=0):
                self.eng, self.s, self.base, self.n = eng, s, base, 0

            def __call__(self, ins):
                ins.then_inc(self.s, 1)
                self.n += 1
                self.eng.wait_ge(self.s, self.base + self.n)

        block = ctx.enter_context(nc.Block())

        @block.sync
        def _(sp):
            rows_in = t["x"][0].rearrange("(t p) d -> p t d", p=P)

            def load_x(j):
                sp.dma_start(x[:, 2 * j:2 * j + 2, :], rows_in[:, 2 * j:2 * j + 2, :]).then_inc(x_in[j], 16)

            wq = t["w_qkv"][0].rearrange("(k p) n -> p k n", p=P)

            def load_wqkv(n):
                sp.dma_start(wqkv_ring[n % 2], wq[:, :, BANK * n:BANK * (n + 1)]).then_inc(wqkv_in[n % 2], 16)

            load_x(0)
            n_params = [0]

            def param(dst, src):
                sp.dma_start(dst, src, allow_slow_non_contiguous=True).then_inc(params_in, 16)
                n_params[0] += 1

            sp.dma_start(const[:], t["const"]).then_inc(first_params_in, 16)
            sp.dma_start(gains[:, 0, :], t["attn_norm"][0].rearrange("(k p) -> p k", p=P),
                         allow_slow_non_contiguous=True).then_inc(first_params_in, 16)
            for j in range(1, 4):
                load_x(j)
            load_wqkv(0)
            param(assignment[:], t["assignment"])
            for j, src in enumerate((t["pool_norm"][0], t["ffn_norm"][0], t["ffn_norm"][1])):
                param(gains[:, j + 1, :], src.rearrange("(k p) -> p k", p=P))
            for c in range(2):
                for n in range(4):
                    param(qk_gain[HD * c:HD * (c + 1), n:n + 1],
                          t["q_gain" if n < 2 else "k_gain"][0].rearrange("(p a) -> p a", a=1))
            param(sub_gain[:], t["subln_gain"][0].rearrange("(p a) -> p a", a=1))
            for j, n in enumerate(("lambda_q1", "lambda_k1", "lambda_q2", "lambda_k2")):
                param(lam_in[j], row_of(t[n], HD))
            param(line_in, t["bias_line"])
            assert n_params[0] == N_PARAMS
            sp.wait_ge(rel_zeroed, 2)
            sp.dma_start(rel[0:BUCKETS, 0:HEADS], t["rel_bias"]).then_inc(rel_in, 16)
            load_wqkv(1)
            sp.wait_ge(line_sb, 1)
            sp.dma_start(line_dram.ap(), line[0:HEADS]).then_inc(line_stored, 16)

            for n in range(2, 6):
                sp.wait_ge(qkv_mm, NT * (n - 1))
                load_wqkv(n)

            sp.wait_ge(line_stored, 16)
            sp.wait_ge(qk_kept, 4 * NT)
            sp.dma_start(strip_flipped, bass.AP(tensor=line_dram, offset=0, ap=[[1, P], [LINE + 1, HEADS], [1, 2 * P]])
                         ).then_inc(strip_in, 16)
            after_phase(sp, "qkv")
            sp.dma_start(wo, t["w_o"][0].rearrange("(k p) n -> p k n", p=P)).then_inc(wo_in, 16)

            def router(l):
                sp.dma_start(w_router[:, :, 0:GROUPS], t["router_group_w"][l].rearrange("(k p) n -> p k n", p=P)
                             ).then_inc(router_in, 16)
                sp.dma_start(w_router[:, :, GROUPS:], t["router_expert_w"][l].rearrange("(k p) n -> p k n", p=P)
                             ).then_inc(router_in, 16)
                sp.dma_start(b_router[:, 0:GROUPS], row_of(t["router_group_b"], GROUPS, l * GROUPS)
                             ).then_inc(router_in, 16)
                sp.dma_start(b_router[:, GROUPS:], row_of(t["router_expert_b"], NE, l * NE)).then_inc(router_in, 16)
                rows = normed_dram[l].rearrange("(t p) d -> p t d", p=P)
                n0 = PAIRS * NORMS.index(f"ffn{l}")
                for i in range(NT):
                    sp.wait_ge(norm_rows_ready[i % 2], n0 + i // 2 + 1)
                    sp.dma_start(rows[:, i, :], normed[i % 2]).then_inc(stored[i % 2], 16)

            def moe(l, before):
                m, once = moe_of[l], l + 1
                after_phase(sp, before)

                def load_weights(e, b, k):
                    src = (t["w_gate"], t["w_up"], t["w_down"])[k][l]
                    src = src[ds(e, 1)].rearrange("a (k p) n -> p (a k) n", p=P) if not isinstance(e, int) else \
                        src[e].rearrange("(k p) n -> p k n", p=P)
                    sp.dma_start(wslot[b][k], src).then_inc(w_in_sem[k][b], 16)

                sp.wait_ge(clear_ready, once)
                sp.dma_start(slots_dram[l].ap().rearrange("(p a) b -> p (a b)", p=P), no_slots
                             ).then_inc(table_cleared, 16)
                for e, k in ((0, 0), (0, 1), (0, 2), (1, 0), (1, 1)):
                    load_weights(e, e, k)
                sp.wait_ge(tabled, 16 * 2 * NT * once)
                sp.dma_start(slot_all, slots_dram[l].ap().rearrange("(j p e) b -> p j (e b)", p=P, e=NE)
                             ).then_inc(table_in, 16)
                sp.wait_ge(lists, once)
                first = [NE // RING * l + (l if j < NE % RING else 0) for j in range(RING)]
                sp.wait_ge(m.rows_in, 16)
                load_weights(1, 1, 2)
                load_weights(2, 2, 0)
                sp.wait_ge(w_in_sem[2][1], 16 * (first[1] + 1))
                load_weights(2, 2, 1)
                sp.wait_ge(w_in_sem[0][2], 16 * (first[2] + 1))
                load_weights(2, 2, 2)

                def next_expert(e, b, turn_of_slot):
                    before, prev = (b - 1) % RING, turn_of_slot - (b == 0)
                    in_flight = [(before, 1, prev), (before, 2, prev), (b, 0, turn_of_slot)]
                    tiles_through = sp.value_load(meta[0:1, ds(e - 2, 1), 1:2], min_val=1, max_val=64)
                    products_through = sp.to_reg(tiles_through * KF)
                    landed = [sp.to_reg(16 * (first[slot] + turn_ + 1)) for slot, _, turn_ in in_flight]
                    for k in range(3):
                        slot, kind, _ = in_flight[k]
                        sp.wait_ge(w_in_sem[kind][slot], landed[k])
                        if k == 0:
                            sp.wait_ge(m.gate_up, products_through)
                        if k == 2:
                            sp.wait_ge(m.down, tiles_through)
                        load_weights(e, b, k)

                with sp.Fori(1, NE // RING) as er:
                    for b in range(RING):
                        next_expert(er * RING + b, b, er)
                for b in range(NE % RING):
                    next_expert(NE // RING * RING + b, b, NE // RING)

            def load_w_in(half):
                sp.dma_start(w_in[:, :, BANK * half:BANK * (half + 1)],
                             t["pool_w_in"][0].rearrange("(k p) n -> p k n", p=P)[:, :, BANK * half:BANK * (half + 1)]
                             ).then_inc(w_in_in[half], 16)

            def pairs_in(l):
                m = moe_of[l]
                tiles = sp.value_load(total[0:1, 0:1], min_val=1, max_val=64)
                sp.wait_ge(m.scattered, tiles * 16 + 48)
                pairs = expert_out_dram[l].rearrange("(t p k) d -> p t k d", p=P, k=2)
                ahead = PAIR_BUFS - 1
                for i in range(NT + ahead):
                    b = i % PAIR_BUFS
                    if PAIR_BUFS <= i < NT:
                        sp.wait_ge(pair_used[b], NT // PAIR_BUFS * l + i // PAIR_BUFS)
                    if i < NT:
                        sp.dma_start(y_pair[b], pairs[:, i]).then_inc(pair_in[b], 16)
                    if l == 0 and i in (PAIR_BUFS - 1, NT - 1):
                        load_w_in(i // PAIR_BUFS)
                    if l == 1 and i >= ahead:
                        store_out(i - ahead)

            def store_out(i):
                sp.wait_ge(pair_used[i % PAIR_BUFS], (NT + i) // PAIR_BUFS + 1)
                sp.dma_start(out[0].rearrange("(t p) d -> p t d", p=P)[:, i, :], x[:, i, :]).then_inc(out_stored, 16)

            after_phase(sp, "attention")
            router(0)
            moe(0, "projection")

            after_phase(sp, "moe0")
            pairs_in(0)
            sp.dma_start(w_grp, t["pool_w_group"][0].rearrange("g (k p) n -> p (g k) n", p=P)).then_inc(pool_in, 16)
            sp.dma_start(w_out, t["pool_w_out"][0].rearrange("(k p) n -> p k n", p=P)).then_inc(pool_in, 16)
            sp.dma_start(scale_row, row_of(t["pool_scale"], D)).then_inc(pool_in, 16)
            sp.wait_ge(pooled, KD)
            router(1)
            moe(1, "pool")
            after_phase(sp, "moe1")
            pairs_in(1)
            sp.wait_ge(out_stored, 16 * NT)

        def norm_act(act, name, i, scratch):
            n = NT * NORMS.index(name) + i
            if n >= 1:
                act.wait_ge(norm_ssq, n)
            nc.scalar.activation(scratch, x[:, i, :], ACT.Square, accum_out=x_ssq[:, i:i + 1]).then_inc(norm_ssq, 1)
            act.wait_ge(norm_ssq, n + 1)
            nc.scalar.activation(x_std[:, i:i + 1], x_ssq[:, i:i + 1], ACT.Sqrt, bias=eps_t, scale=1.0 / D
                                 ).then_inc(norm_std, 1)

        def norm_rows(dve, link, name, i, dst):
            n0, b = NORMS.index(name), i % 2
            dve.wait_ge(norm_std, NT * n0 + i + 1)
            link(nc.vector.reciprocal(x_rstd[:, i:i + 1], x_std[:, i:i + 1]))
            if PAIRS * n0 + i // 2 >= 1:
                dve.wait_ge(norm_turned[b], PAIRS * n0 + i // 2)
            if name[:3] == "ffn" and i >= 2:
                dve.wait_ge(stored[b], 16 * (PAIRS * int(name[3]) + i // 2))
            nc.vector.tensor_scalar(dst[b], x[:, i, :], x_rstd[:, i:i + 1], None, ALU.mult
                                    ).then_inc(norm_rows_ready[b], 1)

        def norm_turn(pe, name, i, src, bank_of):
            n0, b = PAIRS * NORMS.index(name), i % 2
            pe.wait_ge(norm_rows_ready[b], n0 + i // 2 + 1)
            if bank_of(0) == bank_of(1) and i >= 1:
                pe.wait_ge(norm_kept[1 - b], n0 + (i - 1) // 2 + 1)
            elif i >= 2:
                pe.wait_ge(norm_kept[b], n0 + i // 2)
            turn(lambda k: src[b][:, P * k:P * (k + 1)], bank_of(b), KD, norm_turned[b])

        def norm_keep(dve, name, i, bank_of, dst, gain):
            b = i % 2
            dve.wait_ge(norm_turned[b], PAIRS * NORMS.index(name) + i // 2 + 1)
            nc.vector.tensor_tensor(out=dst, in0=bank(bank_of(b), 2).rearrange("p (k q) -> p k q", k=KD),
                                    in1=gain.unsqueeze(2).to_broadcast([P, KD, P]), op=ALU.mult
                                    ).then_inc(norm_kept[b], 1)

        def attn_banks(b):
            return 2 * b

        def ffn_banks(b):
            return 6

        def pool_banks(b):
            return 4 + 2 * b

        def turn(src, dst_bank, n, done):
            for k in range(n):
                last = nc.tensor.transpose(psum[:, BANK * dst_bank + P * k:BANK * dst_bank + P * (k + 1)],
                                           src(k), ident)
            last.then_inc(done, 1)

        @block.tensor
        def _(pe):
            pe.wait_ge(first_params_in, 32)
            for i in range(NT):
                norm_turn(pe, "attn", i, attn_normed, attn_banks)
            pe.wait_ge(params_in, 16 * N_PARAMS)
            pe.wait_ge(rel_in, 16)
            pe.wait_ge(rel_zeroed, 3)
            nc.tensor.matmul(bank(6)[:, 0:LINE + 1], rel, line_in, start=True, stop=True).then_inc(line_psum, 1)
            end_phase(pe, "attn_norm")

            def qk_turn(i, u):
                pe.wait_ge(qk_ready, u + 1 + 1)
                if i >= 0:
                    turn(lambda k: qk_rows[i % 2].rearrange("p a b -> p (a b)")[:, P * k:P * (k + 1)],
                         4 + i % 2, 4, qk_turned)

            with pe.Fori(0, 2) as np_:
                for s in range(2):
                    pe.wait_ge(wqkv_in[s], 16 * np_ + 16)
                    for i in range(NT):
                        u = 16 * np_ + 8 * s + i
                        if i < 2:
                            pe.wait_ge(qk_ready, 16 * np_ + 8 * s + 1)
                        else:
                            pe.wait_ge(qk_ready, u - 1 + 1)
                        for k in range(KD):
                            last = nc.tensor.matmul(bank(i % 2), hT[:, k, P * i:P * (i + 1)], wqkv_ring[s][:, k, :],
                                                    start=k == 0, stop=k == KD - 1)
                        last.then_inc(qkv_mm, 1)
                        if i >= 1:
                            qk_turn(i - 1, u - 1)
                    qk_turn(NT - 1, 16 * np_ + 8 * s + NT - 1)
            for s in range(2):
                pe.wait_ge(wqkv_in[s], 16 * 3)
                for i in range(NT):
                    uv = 8 * s + i
                    if uv == 12:
                        pe.wait_ge(strip_in, 16)
                        pe.wait_ge(qk_kept, 4 * NT)
                        for n in range(4):
                            last = nc.tensor.matmul(bank(4 + n), const[:, C_FLIP:], strip_flipped[:, 2 * n:2 * n + 2, :],
                                                    start=True, stop=True)
                        last.then_inc(strip_turned, 1)
                    if uv >= 2:
                        pe.wait_ge(v_kept, uv - 1)
                    for k in range(KD):
                        last = nc.tensor.matmul(bank(i % 2), hT[:, k, P * i:P * (i + 1)], wqkv_ring[s][:, k, :],
                                                start=k == 0, stop=k == KD - 1)
                    last.then_inc(qkv_mm, 1)
            end_phase(pe, "qkv")

            score_bank, turn_bank, av_bank = (0, 2), 4, (6, 7)

            def att_scores(hp, s, qb, first_use):
                st = 16 * hp + 8 * s + qb
                if qb == 0:
                    pe.wait_ge(staged[s], 2 * hp + 2)
                for c in range(2):
                    if not first_use:
                        pe.wait_ge(exped[c], st)
                    width = P * (qb + 1)
                    for w0 in range(0, width, BANK):
                        w = min(BANK, width - w0)
                        last = nc.tensor.matmul(psum[:, BANK * score_bank[c] + w0:BANK * score_bank[c] + w0 + w],
                                                q_head[s][HD * c:HD * (c + 1), P * qb:P * (qb + 1)],
                                                k_head[s][HD * c:HD * (c + 1), w0:w0 + w], start=True, stop=True)
                    last.then_inc(scores[c], 1)

            def att_av(h, qb, st, par, bank_used):
                pe.wait_ge(p_kept, st + 1)
                if bank_used:
                    pe.wait_ge(o_kept, st - 1)
                for kt in range(qb + 1):
                    last = nc.tensor.matmul(psum[:, BANK * av_bank[par]:BANK * av_bank[par] + P], probT[:, kt, :],
                                            v[:, kt, ds(h * P, P)] if not isinstance(h, int) else
                                            v[:, kt, P * h:P * (h + 1)],
                                            start=kt == 0, stop=kt == qb)
                last.then_inc(av_done, 1)

            def att_turn(qb, st, par, turned_before):
                pe.wait_ge(combined, st + 1)
                if turned_before:
                    pe.wait_ge(p_kept, st)
                turn(lambda k: prob0[par][:, P * k:P * (k + 1)], turn_bank, qb + 1, p_turned)

            def att_pe(hp, first):
                for k in range(16):
                    s, qb = divmod(k, 8)
                    att_scores(hp, s, qb, first and k == 0)
                    if not (first and k < 2):
                        kk = k - 2
                        h = 2 * hp + kk // 8
                        att_av(h, kk % 8, 16 * hp + kk, kk % 2, not (first and k < 4))
                    if not (first and k < 1):
                        kk = k - 1
                        att_turn(kk % 8, 16 * hp + kk, kk % 2, not (first and k < 2))

            pe.wait_ge(strip_kept, 1)
            att_pe(0, True)
            with pe.Fori(1, 4) as hp:
                att_pe(hp, False)
            att_av(7, 6, 62, 0, True)
            att_turn(7, 63, 1, True)
            att_av(7, 7, 63, 1, True)
            end_phase(pe, "attention")

            LOGIT_BANK = 2

            def mixer_out(l, src, weights, ready):
                n0 = PAIRS * NORMS.index(f"ffn{l}")
                for i in range(NT + 2):
                    if l == 0 and i + 1 < NT:
                        turn_o(i + 1)
                    if i < NT:
                        ready(i)
                        for half in range(2):
                            n = 2 * i + half
                            if n >= 2:
                                pe.wait_ge(mixer_added, 2 * NT * l + n - 1)
                            for k in range(KD):
                                last = nc.tensor.matmul(bank(half), src(i, k), weights[:, k, BANK * half:
                                                                                       BANK * (half + 1)],
                                                        start=k == 0, stop=k == KD - 1)
                            last.then_inc(mixer_mm, 1)
                    if 1 <= i <= NT:
                        norm_turn(pe, f"ffn{l}", i - 1, normed, ffn_banks)
                    if i >= 2:
                        j = i - 2
                        if j == 0:
                            pe.wait_ge(router_in, 64 * (l + 1))
                        pe.wait_ge(norm_kept[j % 2], n0 + j // 2 + 1)
                        if j >= 1:
                            pe.wait_ge(biased[(j - 1) % 2], PAIRS * l + (j - 1) // 2 + 1)
                        for k in range(KD):
                            last = nc.tensor.matmul(bank(LOGIT_BANK)[:, 0:GROUPS + NE], rT[j % 2][:, k, :],
                                                    w_router[:, k, :], start=k == 0, stop=k == KD - 1)
                        last.then_inc(logits[j % 2], 1)

            def turn_o(i):
                pe.wait_ge(on_ready, i + 1)
                if i >= 1:
                    pe.wait_ge(oT_kept, i)
                turn(lambda k: o_normed[i % 2][:, k, :], 4, KD, o_turned)

            pe.wait_ge(wo_in, 16)
            turn_o(0)
            mixer_out(0, lambda i, k: oT[i % 2][:, k, :], wo, lambda i: pe.wait_ge(oT_kept, i + 1))
            end_phase(pe, "projection")

            def moe(l):
                m, once = moe_of[l], l + 1
                pe.wait_ge(masks, once)
                nc.tensor.matmul(psum[:, 3072:3072 + 256], tri, t256[3].rearrange("p a b -> p (a b)"),
                                 start=True, stop=True)
                nc.tensor.matmul(psum[:, 3584:3584 + 256], ones[:], t256[3].rearrange("p a b -> p (a b)"),
                                 start=True, stop=True).then_inc(ranks, 1)

                GATE, UP, TURN, DOWN = 0, 2, 4, 6

                def turn_rows(g1):
                    pe.wait_ge(m.rows_in, 16 * g1)
                    turn(lambda k: x_rows[:, P * k:P * (k + 1)], TURN, KD, m.turned)

                pe.wait_ge(lists, once)
                turn_rows(1)

                def expert(e, b, turn_of_slot):
                    wg, wu, wd = wslot[b]
                    loaded = NE // RING * l + (l if b < NE % RING else 0) + turn_of_slot + 1
                    tiles = pe.value_load(meta[0:1, ds(e, 1), 0:1], min_val=1, max_val=8)
                    before = pe.value_load(meta[0:1, ds(e, 1), 1:2], min_val=0, max_val=64)
                    with pe.Fori(0, tiles) as j:
                        g = before + j
                        for k in range(2):
                            pe.wait_ge(w_in_sem[k][b], 16 * loaded)
                        pe.wait_ge(m.xT_kept, g + 1)
                        for f in range(KF):
                            if f >= 2:
                                pe.wait_ge(m.hidden, KF * g + f - 1)
                            for w, at in ((wg, GATE + f % 2), (wu, UP + f % 2)):
                                for k in range(KD):
                                    last = nc.tensor.matmul(psum[:, BANK * at:BANK * at + P],
                                                            w[:, k, P * f:P * (f + 1)], xT[:, k, :],
                                                            start=k == 0, stop=k == KD - 1)
                            last.then_inc(m.gate_up, 1)
                        turn_rows(g + 2)
                        pe.wait_ge(w_in_sem[2][b], 16 * loaded)
                        pe.wait_ge(m.hidden, KF * g + KF)
                        pe.wait_ge(m.y_kept, 2 * g + 3)
                        for half in range(2):
                            for f in range(KF):
                                last = nc.tensor.matmul(bank(DOWN + half), hiddenT[:, f, :],
                                                        wd[:, f, BANK * half:BANK * (half + 1)],
                                                        start=f == 0, stop=f == KF - 1)
                        last.then_inc(m.down, 1)

                with pe.Fori(0, NE // RING) as er:
                    for b in range(RING):
                        expert(er * RING + b, b, er)
                for b in range(NE % RING):
                    expert(NE // RING * RING + b, b, NE // RING)
                end_phase(pe, f"moe{l}")

            moe(0)

            n0 = PAIRS * NORMS.index("pool")

            def u_product(n):
                half, c = divmod(n, KD)
                if c == 0:
                    for b in range(2):
                        pe.wait_ge(norm_kept[b], n0 + 2 * half + 2)
                if n in (0, KD // 2):
                    pe.wait_ge(w_in_in[2 * n // KD], 16)
                if n >= 4:
                    pe.wait_ge(u_kept, n - 3)
                for k in range(KD):
                    last = nc.tensor.matmul(bank(n % 4), w_in[:, k, P * c:P * (c + 1)],
                                            hT[:, k, BANK * half:BANK * (half + 1)],
                                            start=k == 0, stop=k == KD - 1)
                last.then_inc(u_mm, 1)

            for i in range(NT):
                norm_turn(pe, "pool", i, normed, pool_banks)
                if i >= 4:
                    u_product(i - 4)
            for n in range(4, 2 * KD):
                u_product(n)
            pe.wait_ge(pool_in, 48)
            n = 0
            for g in range(len(WINDOWS)):
                pe.wait_ge(pooled, 2 * g + 2)
                for ec in range(2):
                    for half in range(2):
                        if n >= 2:
                            pe.wait_ge(mix_kept, n - 1)
                        for kc in range(2):
                            last = nc.tensor.matmul(bank(4 + n % 2), w_grp[:, 2 * g + kc, P * ec:P * (ec + 1)],
                                                    uT[:, 2 * g + kc, PAD + BANK * half:PAD + BANK * (half + 1)],
                                                    start=kc == 0, stop=kc == 1)
                        last.then_inc(mix_mm, 1)
                        n += 1
            mixer_out(1, lambda i, k: mixedT[:, k, P * i:P * (i + 1)], w_out,
                      lambda i: pe.wait_ge(mix_kept, 16) if i == 0 else None)
            end_phase(pe, "pool")
            moe(1)

        @block.scalar
        def _(act):
            act.wait_ge(rel_zeroed, 3)
            for i in range(NT):
                act.wait_ge(x_in[i // 2], 16)
                norm_act(act, "attn", i, attn_square)
            act.wait_ge(lam_sums, 1)
            nc.scalar.activation(lam_t[:, 2:4], lam_t[:, 0:2], ACT.Exp).then_inc(lam_exp, 1)
            end_phase(act, "attn_norm")

            with act.Fori(0, 2) as np_:
                for k in range(16):
                    u = 16 * np_ + k
                    act.wait_ge(qkv_mm, u + 1)
                    act.wait_ge(qk_ssq, u + 1)
                    nc.scalar.activation(qk_square.rearrange("p a b -> p (a b)"), bank(k % 2), ACT.Square
                                         ).then_inc(qk_sq, 1)
                    act.wait_ge(qk_ssq, u + 1 + 1)
                    nc.scalar.activation(std, ssq, ACT.Sqrt, bias=eps_t, scale=1.0 / HD).then_inc(qk_std, 1)
            act.wait_ge(line_stored, 16)
            for n in range(16):
                act.wait_ge(qkv_mm, 32 + n + 1)
                nc.scalar.activation(v[:, n % 8, BANK * (n // 8):BANK * (n // 8 + 1)], bank(n % 2), ACT.Copy
                                     ).then_inc(v_kept, 1)
            end_phase(act, "qkv")

            def att_exp(hp, k, c, first):
                st, par, width = 16 * hp + k, k % 2, P * (k % 8 + 1)
                act.wait_ge(maxed[c], st + 1)
                if not (first and k < 2) and c == 0:
                    act.wait_ge(p_turned, st - 1)
                if not (first and k < 1) and c == 1:
                    act.wait_ge(combined, st)
                nc.scalar.activation((prob0[par] if c == 0 else prob1)[:, 0:width],
                                     psum[:, BANK * 2 * c:BANK * 2 * c + width], ACT.Exp,
                                     bias=neg_max[:, par, c:c + 1], accum_out=sums[:, par, c:c + 1]
                                     ).then_inc(exped[c], 1)

            def att_keep(st, qb, first):
                act.wait_ge(p_turned, st + 1)
                if not first:
                    act.wait_ge(av_done, st)
                nc.scalar.activation(probT[:, 0:qb + 1, :].rearrange("p a b -> p (a b)"),
                                     psum[:, BANK * 4:BANK * 4 + P * (qb + 1)], ACT.Copy).then_inc(p_kept, 1)

            def att_act(hp, first):
                for k in range(16):
                    for c in range(2):
                        att_exp(hp, k, c, first)
                    if not (first and k < 1):
                        att_keep(16 * hp + k - 1, (k - 1) % 8, first and k < 2)

            att_act(0, True)
            with act.Fori(1, 4) as hp:
                att_act(hp, False)
            att_keep(63, 7, False)
            end_phase(act, "attention")

            for i in range(-2, NT):
                j = i + 2
                if j < NT:
                    if j >= 1:
                        act.wait_ge(o_ssq, j)
                    nc.scalar.activation(o_square, o_rows[:, :, P * j:P * (j + 1)], ACT.Square).then_inc(o_sq, 1)
                    act.wait_ge(o_ssq, j + 1)
                    nc.scalar.activation(std, ssq, ACT.Sqrt, bias=eps_t, scale=1.0 / P).then_inc(o_std, 1)
                if i >= 0:
                    act.wait_ge(mixer_added, 2 * i + 2)
                    norm_act(act, "ffn0", i, square)
            end_phase(act, "projection")

            def moe(l):
                m, once = moe_of[l], l + 1
                act.wait_ge(act_in, 2 * l + 1)
                nc.scalar.activation(t32[1].rearrange("p a b -> p (a b)"), t32[0].rearrange("p a b -> p (a b)"),
                                     ACT.Exp).then_inc(act_out, 1)
                act.wait_ge(act_in, 2 * l + 2)
                nc.scalar.activation(t8[:, 7, :], t8[:, 6, :], ACT.Exp).then_inc(act_out, 1)
                act.wait_ge(lists, once)
                tiles = act.value_load(total[0:1, 0:1], min_val=1, max_val=64)
                with act.Fori(0, tiles) as g:
                    for f in range(KF):
                        act.wait_ge(m.gate_up, KF * g + f + 1)
                        nc.scalar.activation(gated[:, f, :], bank(f % 2)[:, 0:P], ACT.Silu).then_inc(m.silu, 1)
                    act.wait_ge(m.down, g + 1)
                    act.wait_ge(m.scattered, 16 * g + 48)
                    nc.scalar.activation(y_rows[:, 0:BANK], bank(6), ACT.Copy).then_inc(m.y_kept, 1)
                end_phase(act, f"moe{l}")

            moe(0)
            for i in range(NT):
                act.wait_ge(pair_used[i % PAIR_BUFS], i // PAIR_BUFS + 1)
                norm_act(act, "pool", i, square)
            act.wait_ge(pads, 1)
            for n in range(2 * KD):
                half, c = divmod(n, KD)
                act.wait_ge(u_mm, n + 1)
                nc.scalar.activation(uT[:, c, PAD + BANK * half:PAD + BANK * (half + 1)], bank(n % 4), ACT.Copy
                                     ).then_inc(u_kept, 1)
            for n in range(16):
                c, half = divmod(n, 2)
                act.wait_ge(mix_mm, n + 1)
                nc.scalar.activation(mixedT[:, c, BANK * half:BANK * (half + 1)], bank(4 + n % 2), ACT.Copy
                                     ).then_inc(mix_kept, 1)
            for i in range(NT):
                act.wait_ge(mixer_added, 2 * NT + 2 * i + 2)
                norm_act(act, "ffn1", i, square)
            end_phase(act, "pool")
            moe(1)

        @block.vector
        def _(dve):
            link = Link(dve, dve_link)
            nc.vector.memset(rel, 0.0).then_inc(rel_zeroed, 1)
            dve.wait_ge(rel_zeroed, 1)
            nc.vector.memset(rel[BUCKETS:BUCKETS + 1, 0:HEADS], MASKED).then_inc(rel_zeroed, 1)
            nc.vector.memset(eps_t, EPS)
            nc.vector.memset(ones[:], 1.0).then_inc(rel_zeroed, 1)
            dve.wait_ge(first_params_in, 32)
            for i in range(NT + 1):
                if i < NT:
                    norm_rows(dve, link, "attn", i, attn_normed)
                if i >= 1:
                    norm_keep(dve, "attn", i - 1, attn_banks, hT[:, :, P * (i - 1):P * i], gains[:, 0, :])
            dve.wait_ge(params_in, 16 * N_PARAMS)
            link(nc.vector.tensor_tensor(out=lam_prod[:, 0, :], in0=lam_in[0], in1=lam_in[1], op=ALU.mult))
            link(nc.vector.tensor_tensor(out=lam_prod[:, 1, :], in0=lam_in[2], in1=lam_in[3], op=ALU.mult))
            nc.vector.tensor_reduce(out=lam_t[:, 0:2], in_=lam_prod, axis=AX.X, op=ALU.add).then_inc(lam_sums, 1)
            nc.vector.tensor_scalar(qk_gain[:, 0:2], qk_gain[:, 0:2], HD ** -0.5, None, ALU.mult)
            nc.vector.tensor_scalar(sub_gain[:], sub_gain[:], 1.0 - LAMBDA_INIT, None, ALU.mult)
            dve.wait_ge(line_psum, 1)
            nc.vector.tensor_copy(line[0:HEADS], bank(6)[0:HEADS, 0:LINE + 1]).then_inc(line_sb, 1)
            dve.wait_ge(lam_exp, 1)
            link(nc.vector.tensor_tensor(out=lam_t[:, 4:5], in0=lam_t[:, 3:4], in1=lam_t[:, 2:3], op=ALU.subtract))
            link(nc.vector.tensor_scalar(neg_lam, lam_t[:, 4:5], -LAMBDA_INIT, None, ALU.add))
            end_phase(dve, "attn_norm")

            with dve.Fori(0, 2) as np_:
                chunk_link = Link(dve, qk_link, np_ * 16)
                for k in range(16):
                    u = 16 * np_ + k
                    dve.wait_ge(qk_sq, u + 1)
                    nc.vector.tensor_reduce(out=ssq, in_=qk_square, axis=AX.X, op=ALU.add).then_inc(qk_ssq, 1)
                    dve.wait_ge(qk_std, u + 1)
                    chunk_link(nc.vector.reciprocal(rstd, std))
                    nc.vector.tensor_tensor(out=qk_rows[k % 2], in0=bank(k % 2).rearrange("p (a b) -> p a b", a=8),
                                            in1=rstd.unsqueeze(2).to_broadcast([P, 8, HD]), op=ALU.mult
                                            ).then_inc(qk_ready, 1)
                    dve.wait_ge(qk_turned, u + 1)
                    n = 2 * np_ + k // 8
                    nc.vector.tensor_scalar(qkT[:, ds(n * 4, 4), P * (k % 8):P * (k % 8 + 1)],
                                            bank(4 + k % 2).rearrange("p (a b) -> p a b", a=4),
                                            qk_gain[:, ds(n, 1)], None, ALU.mult).then_inc(qk_kept, 1)
            dve.wait_ge(strip_turned, 1)
            nc.vector.tensor_copy(strip, bank(4, 4).rearrange("p (h k) -> p h k", h=HEADS)).then_inc(strip_kept, 1)
            end_phase(dve, "qkv")

            dve.wait_ge(strip_kept, 1)

            def att_prep(hp, k, c, al):
                st, s, qb = 16 * hp + k, k // 8, k % 8
                near = P * min(qb + 1, 2)
                end = BANK * 2 * c + P * (qb + 1)
                dve.wait_ge(scores[c], st + 1)
                h = 2 * hp + s
                al(nc.vector.tensor_tensor(out=psum[:, end - near:end], in0=psum[:, end - near:end],
                                           in1=(strip[:, h, 2 * P - near:] if isinstance(h, int) else
                                                strip[:, ds(h, 1), 2 * P - near:].rearrange("p a b -> p (a b)")),
                                           op=ALU.add))
                nc.vector.tensor_reduce(out=neg_max[:, k % 2, c:c + 1], in_=psum[:, BANK * 2 * c:end], axis=AX.X,
                                        op=ALU.max, negate=True).then_inc(maxed[c], 1)

            def att_combine(st, par, qb, al):
                for c in range(2):
                    dve.wait_ge(exped[c], st + 1)
                al(nc.vector.reciprocal(rsum[:, par, :], sums[:, par, :]))
                al(nc.vector.tensor_scalar(coef[:, par:par + 1], sums[:, par, 0:1], rsum[:, par, 1:2], neg_lam,
                                           ALU.mult, ALU.mult))
                w = P * (qb + 1)
                nc.vector.scalar_tensor_tensor(out=prob0[par][:, 0:w], in0=prob1[:, 0:w], scalar=coef[:, par:par + 1],
                                               in1=prob0[par][:, 0:w], op0=ALU.mult, op1=ALU.add
                                               ).then_inc(combined, 1)

            def att_out(h, st, par, qb):
                dve.wait_ge(av_done, st + 1)
                dst = (o_rows[:, h, P * qb:P * (qb + 1)] if isinstance(h, int) else
                       o_rows[:, ds(h, 1), P * qb:P * (qb + 1)].rearrange("p a b -> p (a b)"))
                nc.vector.tensor_scalar(dst, psum[:, BANK * (6 + par):BANK * (6 + par) + P], rsum[:, par, 0:1], None,
                                        ALU.mult).then_inc(o_kept, 1)

            def att_dve(hp, first, al):
                for k in range(16):
                    att_prep(hp, k, 0, al)
                    if not (first and k < 1):
                        att_combine(16 * hp + k - 1, (k - 1) % 2, (k - 1) % 8, al)
                    att_prep(hp, k, 1, al)
                    if not (first and k < 2):
                        kk = k - 2
                        att_out(2 * hp + kk // 8, 16 * hp + kk, kk % 2, kk % 8)

            al = Link(dve, att_link)
            att_dve(0, True, al)
            assert al.n == 16 * 4 - 2
            with dve.Fori(1, 4) as hp:
                al = Link(dve, att_link, hp * 64 - 2)
                att_dve(hp, False, al)
                assert al.n == 64
            al = Link(dve, att_link, 4 * 64 - 2)
            att_out(7, 62, 0, 6)
            dve.wait_ge(o_kept, 63)
            att_combine(63, 1, 7, al)
            att_out(7, 63, 1, 7)
            end_phase(dve, "attention")

            def o_norm(i):
                dve.wait_ge(o_sq, i + 1)
                nc.vector.tensor_reduce(out=ssq, in_=o_square, axis=AX.X, op=ALU.add).then_inc(o_ssq, 1)
                dve.wait_ge(o_std, i + 1)
                link(nc.vector.reciprocal(rstd, std))
                if i >= 2:
                    dve.wait_ge(o_turned, i - 1)
                nc.vector.tensor_tensor(out=o_normed[i % 2], in0=o_rows[:, :, P * i:P * (i + 1)],
                                        in1=rstd.unsqueeze(2).to_broadcast([P, HEADS, P]), op=ALU.mult
                                        ).then_inc(on_ready, 1)

            def keep_o(i):
                dve.wait_ge(o_turned, i + 1)
                if i >= 2:
                    dve.wait_ge(mixer_mm, 2 * i - 2)
                nc.vector.tensor_scalar(oT[i % 2].rearrange("p a b -> p (a b)"), bank(4, 2), sub_gain[:, 0:1],
                                        None, ALU.mult).then_inc(oT_kept, 1)

            def mixer_out(l):
                name = f"ffn{l}"
                for i in range(NT + 2):
                    if l == 0 and i + 2 < NT:
                        o_norm(i + 2)
                    if l == 0 and i + 1 < NT:
                        keep_o(i + 1)
                    if i < NT:
                        for half in range(2):
                            n = 2 * NT * l + 2 * i + half
                            dve.wait_ge(mixer_mm, n + 1)
                            part = slice(BANK * half, BANK * (half + 1))
                            if l == 0:
                                add = bank(half)
                            else:
                                if i >= 1:
                                    dve.wait_ge(mixer_added, n - 1)
                                nc.vector.tensor_tensor(out=out_scaled[:, part], in0=bank(half),
                                                        in1=scale_row[:, part], op=ALU.mult
                                                        ).then_inc(mixer_scaled, 1)
                                dve.wait_ge(mixer_scaled, 2 * i + half + 1)
                                add = out_scaled[:, part]
                            nc.vector.tensor_tensor(out=x[:, i, part], in0=add, in1=x[:, i, part], op=ALU.add
                                                    ).then_inc(mixer_added, 1)
                        norm_rows(dve, link, name, i, normed)
                    if 1 <= i <= NT:
                        j = i - 1
                        if j >= 2:
                            dve.wait_ge(logits[j % 2], PAIRS * l + j // 2)
                        norm_keep(dve, name, j, ffn_banks, rT[j % 2], gains[:, 2 + l, :])
                    if i >= 2:
                        j = i - 2
                        if j == 0:
                            dve.wait_ge(router_in, 64 * (l + 1))
                        dve.wait_ge(logits[j % 2], PAIRS * l + j // 2 + 1)
                        nc.vector.tensor_tensor(out=logit[:, j, :], in0=bank(2)[:, 0:GROUPS + NE], in1=b_router,
                                                op=ALU.add).then_inc(biased[j % 2], 1)

            o_norm(0)
            o_norm(1)
            keep_o(0)
            mixer_out(0)
            end_phase(dve, "projection")

            def moe(l):
                m, once = moe_of[l], l + 1
                gain = gains[:, 2 + l, :]
                nc.vector.memset(no_slots, NO_SLOT).then_inc(clear_ready, 1)
                for b in range(2):
                    dve.wait_ge(biased[b], PAIRS * once)

                r = link
                iota4 = const[:, C_IOTA4:C_IOTA4 + GROUPS].unsqueeze(1).to_broadcast([P, NT, GROUPS])
                iota32 = const[:, C_IOTA32:C_IOTA32 + NE].unsqueeze(1).to_broadcast([P, NT, NE])
                grp, exp_l = logit[:, :, 0:GROUPS], logit[:, :, GROUPS:]
                gmax, gsum, gp, gi, v1, v2, dv, ed, i1, i2, ta, tb = (t8[:, j, :] for j in range(12))

                def over(a, n):
                    return a.unsqueeze(2).to_broadcast([P, NT, n])

                def tt(o, a, b, op):
                    r(nc.vector.tensor_tensor(out=o, in0=a, in1=b, op=op))

                def red(o, a, op):
                    r(nc.vector.tensor_reduce(out=o, in_=a, axis=AX.X, op=op))

                red(gmax, grp, ALU.max)
                nc.vector.tensor_tensor(out=t32[0], in0=grp, in1=over(gmax, GROUPS), op=ALU.subtract
                                        ).then_inc(act_in, 1)
                dve.wait_ge(act_out, 2 * l + 1)
                red(gsum, t32[1], ALU.add)
                r(nc.vector.reciprocal(gp, gsum))
                tt(t32[2], grp, over(gmax, GROUPS), ALU.is_equal)
                tt(t32[3], t32[2], iota4, ALU.mult)
                red(gi, t32[3], ALU.min)
                tt(t32[2], iota4, over(gi, GROUPS), ALU.is_equal)
                r(nc.vector.tensor_scalar(t32[3], t32[2], BIG, -BIG, ALU.mult, ALU.add))
                el = t256[0]
                tt(el.rearrange("p t (g e) -> p t g e", g=GROUPS), exp_l.rearrange("p t (g e) -> p t g e", g=GROUPS),
                   t32[3].unsqueeze(3).to_broadcast([P, NT, GROUPS, PER_GROUP]), ALU.add)
                one, two = t256[1], t256[2]

                def pick(vmax, idx, hot, tmp):
                    red(vmax, el, ALU.max)
                    tt(tmp, el, over(vmax, NE), ALU.is_equal)
                    tt(tmp, tmp, iota32, ALU.mult)
                    red(idx, tmp, ALU.min)
                    tt(hot, iota32, over(idx, NE), ALU.is_equal)

                pick(v1, i1, one, t256[4])
                r(nc.vector.scalar_tensor_tensor(out=el.rearrange("p a b -> p (a b)"),
                                                 in0=one.rearrange("p a b -> p (a b)"), scalar=-BIG,
                                                 in1=el.rearrange("p a b -> p (a b)"), op0=ALU.mult, op1=ALU.add))
                pick(v2, i2, two, t256[4])
                nc.vector.tensor_tensor(out=t256[3], in0=one, in1=two, op=ALU.add).then_inc(masks, 1)
                nc.vector.tensor_tensor(out=dv, in0=v2, in1=v1, op=ALU.subtract).then_inc(act_in, 1)
                dve.wait_ge(act_out, 2 * l + 2)
                r(nc.vector.tensor_scalar(ta, ed, 1.0, None, ALU.add))
                r(nc.vector.reciprocal(tb, ta))
                r(nc.vector.tensor_tensor(out=gate_w[:, :, 0], in0=tb, in1=gp, op=ALU.mult))
                r(nc.vector.tensor_tensor(out=gate_w[:, :, 1], in0=gate_w[:, :, 0], in1=ed, op=ALU.mult))
                dve.wait_ge(ranks, once)
                before, in_tile, pos = t256[4], t256[5], t256[6]
                r(nc.vector.tensor_copy(in_tile, psum[:, 3584:3584 + 256].rearrange("p (a b) -> p a b", a=NT)))
                r(nc.vector.memset(before[:, 0, :], 0.0))
                for i in range(1, NT):
                    r(nc.vector.tensor_tensor(out=before[:, i, :], in0=before[:, i - 1, :], in1=in_tile[:, i - 1, :],
                                              op=ALU.add))
                cnt, ntile, upto, tmpc = (counts[:, j, :] for j in range(4))
                r(nc.vector.tensor_tensor(out=cnt, in0=before[:, NT - 1, :], in1=in_tile[:, NT - 1, :], op=ALU.add))
                tt(pos, before, psum[:, 3072:3072 + 256].rearrange("p (a b) -> p a b", a=NT), ALU.add)
                for k, (hot, idx) in enumerate(((one, i1), (two, i2))):
                    tt(t256[5], hot, pos, ALU.mult)
                    red(ta, t256[5], ALU.add)
                    r(nc.vector.tensor_scalar(ta, ta, float(NE), IDX0, ALU.mult, ALU.add))
                    tt(tb, ta, idx, ALU.add)
                    nc.vector.tensor_copy(dest[:, :, k], tb).then_inc(dests, 1)
                    dve.wait_ge(dests, 2 * l + k + 1)
                full = t256[5].rearrange("p a b -> p (a b)")[0:1, 0:7 * NE].rearrange("p (e j) -> p e j", e=NE)
                r(nc.vector.tensor_tensor(out=full, in0=cnt[0:1].unsqueeze(2).to_broadcast([1, NE, 7]),
                                          in1=const[0:1, C_THR:C_THR + 7].unsqueeze(1).to_broadcast([1, NE, 7]),
                                          op=ALU.is_gt))
                r(nc.vector.tensor_reduce(out=ntile[0:1], in_=full, axis=AX.X, op=ALU.add))
                r(nc.vector.tensor_scalar(ntile[0:1], ntile[0:1], 1.0, None, ALU.add))
                r(nc.vector.tensor_tensor_scan(out=upto[0:1], data0=ones[0:1, 0:NE], data1=ntile[0:1], initial=0.0,
                                               op0=ALU.mult, op1=ALU.add))
                r(nc.vector.tensor_tensor(out=tmpc[0:1], in0=upto[0:1], in1=ntile[0:1], op=ALU.subtract))
                r(nc.vector.tensor_copy(meta[0:1, :, 0], ntile[0:1]))
                r(nc.vector.tensor_copy(meta[0:1, :, 1], tmpc[0:1]))
                r(nc.vector.tensor_copy(meta[0:1, :, 2], cnt[0:1]))
                r(nc.vector.tensor_copy(total[:], upto[0:1, NE - 1:NE]))
                nc.vector.memset(view(E0, 2, D), 0.0)
                dve.wait_ge(table_in, 16 * once)
                nc.vector.tensor_scalar(gather_all, slot_all, 1, None, ALU.arith_shift_right).then_inc(lists, 1)

                dve.wait_ge(lists, once)
                tiles = dve.value_load(total[0:1, 0:1], min_val=1, max_val=64)

                def keep_rows(g1):
                    dve.wait_ge(m.turned, g1 + 1)
                    nc.vector.tensor_tensor(out=xT, in0=bank(4, 2).rearrange("p (k q) -> p k q", k=KD),
                                            in1=gain.unsqueeze(2).to_broadcast([P, KD, P]), op=ALU.mult
                                            ).then_inc(m.xT_kept, 1)

                keep_rows(1)
                with dve.Fori(0, tiles) as g:
                    for f in range(KF):
                        dve.wait_ge(m.silu, KF * g + f + 1)
                        nc.vector.tensor_tensor(out=hiddenT[:, f, :], in0=gated[:, f, :],
                                                in1=bank(2 + f % 2)[:, 0:P], op=ALU.mult
                                                ).then_inc(m.hidden, 1)
                    keep_rows(g + 2)
                    dve.wait_ge(m.down, g + 1)
                    dve.wait_ge(m.scattered, 16 * g + 48)
                    nc.vector.tensor_copy(y_rows[:, BANK:], bank(7)).then_inc(m.y_kept, 1)

                end_phase(dve, f"moe{l}")

            def combine(l, i):
                b = i % PAIR_BUFS
                dve.wait_ge(pair_in[b], 16 * ((NT * l + i) // PAIR_BUFS + 1))
                nc.vector.scalar_tensor_tensor(out=x[:, i, :], in0=y_pair[b][:, 0, :], scalar=gate_w[:, i, 0:1],
                                               in1=x[:, i, :], op0=ALU.mult, op1=ALU.add).then_inc(sum_link, 1)
                dve.wait_ge(sum_link, NT * l + i + 1)
                nc.vector.scalar_tensor_tensor(out=x[:, i, :], in0=y_pair[b][:, 1, :], scalar=gate_w[:, i, 1:2],
                                               in1=x[:, i, :], op0=ALU.mult, op1=ALU.add
                                               ).then_inc(pair_used[b], 1)

            moe(0)
            for i in range(NT + 2):
                if i < NT:
                    combine(0, i)
                if 1 <= i <= NT:
                    norm_rows(dve, link, "pool", i - 1, normed)
                if i >= 2:
                    norm_keep(dve, "pool", i - 2, pool_banks, hT[:, :, P * (i - 2):P * (i - 1)], gains[:, 1, :])

            for j in range(2):
                nc.vector.memset(win[j][:, 0:PAD], 0.0)
            nc.vector.memset(uT[:, :, 0:PAD], 0.0).then_inc(pads, 1)
            pl = Link(dve, pool_link)
            for c in range(KD):
                w = WINDOWS[c // 2]
                dve.wait_ge(u_kept, KD + c + 1)
                cur, step, j = uT[:, c, :], 1, 0
                while step < w:
                    pl(nc.vector.tensor_tensor(out=win[j][:, PAD:], in0=cur[:, PAD:], in1=cur[:, PAD - step:UW - step],
                                               op=ALU.add))
                    cur, step, j = win[j], 2 * step, 1 - j
                head = small[:, 48:64]
                pl(nc.vector.tensor_tensor(out=head, in0=cur[:, PAD:2 * PAD],
                                           in1=const[:, C_CNT + PAD * (c // 2):C_CNT + PAD * (c // 2 + 1)],
                                           op=ALU.mult))
                pl(nc.vector.scalar_tensor_tensor(out=uT[:, c, 2 * PAD:], in0=cur[:, 2 * PAD:], scalar=1.0 / w,
                                                  in1=uT[:, c, 2 * PAD:], op0=ALU.mult, op1=ALU.subtract))
                nc.vector.tensor_tensor(out=uT[:, c, PAD:2 * PAD], in0=head, in1=uT[:, c, PAD:2 * PAD],
                                        op=ALU.subtract).then_inc(pooled, 1)
            dve.wait_ge(pool_in, 48)
            mixer_out(1)
            end_phase(dve, "pool")
            moe(1)
            for i in range(NT):
                combine(1, i)

        @block.gpsimd
        def _(pool):
            last_token = pool.to_reg(S - 1)
            last_assignment = pool.to_reg(2 * S - 1)
            for s, n in CREDITS:
                pool.sem_inc(s, n)
            end_phase(pool, "attn_norm")
            def stage_pair(hp, first, which=(0, 1)):
                for s in which:
                    h = 2 * hp + s
                    if not first:
                        pool.wait_ge(scores[1], NT * (h - 1))
                    for dst, head in ((q_head[s], h), (k_head[s], h + HEADS)):
                        nc.gpsimd.tensor_copy(dst, qkT[:, ds(head, 1), :].rearrange("p a b -> p (a b)")
                                              ).then_inc(staged[s], 1)

            pool.wait_ge(qk_kept, 4 * NT)
            pool.wait_ge(qkv_mm, 5 * NT)
            stage_pair(0, True, (0,))
            end_phase(pool, "qkv")
            stage_pair(0, True, (1,))
            with pool.Fori(1, HEADS // 2) as hp:
                stage_pair(hp, False)
            end_phase(pool, "attention")
            end_phase(pool, "projection")

            def moe(l):
                m, once = moe_of[l], l + 1
                pool.wait_ge(clear_ready, once)
                for empty in (scatter_now, *scatter_next):
                    nc.gpsimd.tensor_copy(empty[:], no_slots[:, 0:1]).then_inc(m.pool_link, 1)
                pool.wait_ge(m.pool_link, 3)
                nc.gpsimd.indirect_dma_start(
                    out=expert_out_dram[l],
                    out_offset=bass.IndirectOffsetOnAxis(ap=scatter_now[:, 0:1], axis=0), in_=x[:, 0, :],
                    in_offset=None, bounds_check=last_assignment, oob_is_err=False).then_inc(m.scattered, 16)
                pool.wait_ge(table_cleared, 16 * once)
                for k in range(2):
                    pool.wait_ge(dests, 2 * l + k + 1)
                    for i in range(NT):
                        nc.gpsimd.indirect_dma_start(
                            out=slots_dram[l].ap(),
                            out_offset=bass.IndirectOffsetOnAxis(ap=dest[:, i, k:k + 1], axis=0),
                            in_=assignment[:, 2 * i + k:2 * i + k + 1], in_offset=None).then_inc(tabled, 16)
                for b in range(2):
                    pool.wait_ge(stored[b], 16 * PAIRS * once)

                def gather(filled):
                    filled = pool.to_reg(filled)
                    pool.wait_ge(lists, once)
                    pool.wait_ge(m.pool_link, filled)
                    nc.gpsimd.indirect_dma_start(
                        out=x_rows, out_offset=None, in_=normed_dram[l],
                        in_offset=bass.IndirectOffsetOnAxis(ap=gather_now[:, 0:1], axis=0),
                        bounds_check=last_token, oob_is_err=False).then_inc(m.rows_in, 16)

                def scatter(filled, kept):
                    filled, kept = pool.to_reg(filled), pool.to_reg(kept)
                    pool.wait_ge(lists, once)
                    pool.wait_ge(m.pool_link, filled)
                    pool.wait_ge(m.y_kept, kept)
                    nc.gpsimd.indirect_dma_start(
                        out=expert_out_dram[l],
                        out_offset=bass.IndirectOffsetOnAxis(ap=scatter_now[:, 0:1], axis=0), in_=y_rows,
                        in_offset=None, bounds_check=last_assignment, oob_is_err=False).then_inc(m.scattered, 16)

                def next_list(dst, src, sem_, count):
                    count = pool.to_reg(count)
                    pool.wait_ge(lists, once)
                    pool.wait_ge(sem_, count)
                    nc.gpsimd.tensor_copy(dst[:], src).then_inc(m.pool_link, 1)

                pool.wait_ge(lists, once)
                with pool.Fori(0, NE) as e:
                    tiles = pool.value_load(meta[0:1, ds(e, 1), 0:1], min_val=1, max_val=8)
                    before = pool.value_load(meta[0:1, ds(e, 1), 1:2], min_val=0, max_val=64)
                    with pool.Fori(0, tiles) as j:
                        g = before + j
                        pool.wait_ge(m.turned, g + 1)
                        nc.gpsimd.tensor_copy(gather_now[:], gather_all[:, ds(j, 1), ds(e, 1)].rearrange(
                            "p a b -> p (a b)")).then_inc(m.pool_link, 1)
                        gather(4 * g + 4)
                        next_list(scatter_now, scatter_next[0][:], m.scattered, 16 * g + 16)
                        scatter(4 * g + 5, 2 * g + 1)
                        nc.gpsimd.tensor_copy(scatter_next[0][:], scatter_next[1][:]).then_inc(m.pool_link, 1)
                        next_list(scatter_next[1], slot_all[:, ds(j, 1), ds(e, 1)].rearrange("p a b -> p (a b)"),
                                  m.pool_link, 4 * g + 6)
                last = pool.value_load(total[0:1, 0:1], min_val=1, max_val=64)
                pool.wait_ge(m.turned, last + 1)
                gather(4 * last + 3)
                next_list(scatter_now, scatter_next[0][:], m.scattered, 16 * last + 16)
                scatter(4 * last + 4, 2 * last + 1)
                next_list(scatter_now, scatter_next[1][:], m.scattered, 16 * last + 32)
                scatter(4 * last + 5, 2 * last + 3)
                end_phase(pool, f"moe{l}")

            moe(0)
            end_phase(pool, "pool")
            moe(1)


_INS = ["x", "rel_bias", "attn_norm", "w_qkv", "q_gain", "k_gain", "lambda_q1", "lambda_k1", "lambda_q2",
        "lambda_k2", "subln_gain", "w_o", "pool_norm", "pool_w_in", "pool_w_group", "pool_w_out", "pool_scale",
        "ffn_norm", "router_group_w", "router_group_b", "router_expert_w", "router_expert_b", "w_gate", "w_up",
        "w_down"]


def kernel(**inputs):
    import numpy as _np
    import concourse.bacc as _bacc
    from concourse import mybir as _mybir
    from concourse.bass_utils import run_bass_kernel_spmd as _run

    nc = _bacc.Bacc("TRN2", target_bir_lowering=False, num_devices=1)
    arrays, aps = {}, {}
    given = {name: _np.ascontiguousarray(inputs[name]) for name in _INS}
    given["const"] = float_constants()
    given["bias_line"] = bias_line_constants()
    given["assignment"] = int_constants()
    for name, a in given.items():
        arrays[f"in_{name}"] = a
        aps[name] = nc.dram_tensor(f"in_{name}", a.shape, _mybir.dt.from_np(a.dtype), kind="ExternalInput").ap()
    out = nc.dram_tensor("out", (1, S, D), _mybir.dt.float32, kind="ExternalOutput").ap()
    hybrid_trunk_kernel(nc, aps, out)
    r = _run(nc, [arrays], core_ids=[0])
    return r.results[0]["out"]
```
